# Optimizing a Trainium2 kernel written in Bass

```python
import math
import jax, jax.numpy as jnp
from jax import lax
import numpy as np

D_MODEL = 1024
BATCH = 1
SEQ = 1024
DEPTH = 1

HEAD_DIM = 64
D_MIX = D_MODEL
N_HEADS_A = 8
N_HEADS_B = 8
WIDTH_A = N_HEADS_A * HEAD_DIM
WIDTH_B = N_HEADS_B * HEAD_DIM
ROT_DIM = HEAD_DIM // 4
ROPE_THETA = 500000.0
DILATED_PATTERNS = ((128, 1), (512, 4), (2048, 16))
WIN_BLOCK = 128
KV_LATENT = 128
IDX_HEADS = 4
IDX_DIM = 64
TOPK_MAX = 256
Q_BLOCK = 128
EPS = 1e-6
IN_SPLITS = (WIDTH_A, WIDTH_A, WIDTH_A, WIDTH_A,
             WIDTH_B, KV_LATENT, WIDTH_B,
             IDX_HEADS * IDX_DIM, IDX_DIM, IDX_HEADS)
D_IN = sum(IN_SPLITS)

kernel_name = "hybrid_dilated_window_dsa_parallel_heads"

def rmsnorm(x, g):
    xf = x.astype(jnp.float32)
    y = xf * lax.rsqrt(jnp.mean(xf * xf, axis=-1, keepdims=True) + EPS)
    return (y * g.astype(jnp.float32)).astype(x.dtype)

def rope_tables(positions):
    inv_freq = ROPE_THETA ** (-jnp.arange(0, ROT_DIM, 2, dtype=jnp.float32) / ROT_DIM)
    ang = positions.astype(jnp.float32)[..., None] * inv_freq
    return jnp.cos(ang), jnp.sin(ang)

def apply_rope(x, cos, sin):
    half = ROT_DIM // 2
    xr = x[..., :ROT_DIM].astype(jnp.float32)
    x1, x2 = xr[..., :half], xr[..., half:]
    rot = jnp.concatenate([x1 * cos - x2 * sin, x2 * cos + x1 * sin], axis=-1)
    return jnp.concatenate([rot.astype(x.dtype), x[..., ROT_DIM:]], axis=-1)

def split_columns(proj):
    offs = [int(v) for v in np.cumsum(IN_SPLITS)[:-1]]
    return jnp.split(proj, offs, axis=-1)

def dilated_window_pattern(q, k, v, dilation, steps):
    B, S, H, D = q.shape
    n = S // dilation
    nb = -(-n // WIN_BLOCK)
    npad = nb * WIN_BLOCK

    def to_sub(t):
        t = t.reshape(B, n, dilation, H, D)
        return jnp.pad(t, ((0, 0), (0, npad - n), (0, 0), (0, 0), (0, 0)))

    def band(t):
        tp = jnp.pad(t, ((0, 0), (WIN_BLOCK, 0), (0, 0), (0, 0), (0, 0)))
        tp = tp.reshape(B, nb + 1, WIN_BLOCK, dilation, H, D)
        return jnp.concatenate([tp[:, :-1], tp[:, 1:]], axis=2)

    qb = to_sub(q).reshape(B, nb, WIN_BLOCK, dilation, H, D)
    kb = band(to_sub(k))
    vb = band(to_sub(v))
    s = jnp.einsum('bnqrhd,bnkrhd->bnrhqk', qb, kb).astype(jnp.float32) * (D ** -0.5)
    qi = jnp.arange(WIN_BLOCK)[:, None]
    kj = jnp.arange(2 * WIN_BLOCK)[None, :]
    diff = qi + WIN_BLOCK - kj
    key_step = jnp.arange(nb)[:, None, None] * WIN_BLOCK - WIN_BLOCK + kj[None]
    mask = (diff >= 0) & (diff <= steps) & (key_step >= 0)
    s = jnp.where(mask[None, :, None, None], s, -jnp.inf)
    m = jnp.max(s, axis=-1, keepdims=True)
    p = jnp.exp(s - m)
    l = jnp.sum(p, axis=-1, keepdims=True)
    o = jnp.einsum('bnrhqk,bnkrhd->bnqrhd', (p / l).astype(v.dtype), vb)
    lse = (m + jnp.log(l))[..., 0]
    o = o.reshape(B, npad, dilation, H, D)[:, :n].reshape(B, S, H, D)
    lse = lse.transpose(0, 1, 4, 2, 3).reshape(B, npad, dilation, H)[:, :n].reshape(B, S, H)
    return o, lse

def dilated_mixture(q, k, v):
    outs, lses = [], []
    for window, dilation in DILATED_PATTERNS:
        o, lse = dilated_window_pattern(q, k, v, dilation, window // dilation)
        outs.append(o)
        lses.append(lse)
    alpha = jax.nn.softmax(jnp.stack(lses, axis=-1), axis=-1)
    o = jnp.stack(outs, axis=-1).astype(jnp.float32)
    return jnp.einsum('bshdp,bshp->bshd', o, alpha).astype(q.dtype)

def indexed_sparse_attention(q, k, latent, iq, ik, iw):
    B, S, HB, D = q.shape
    n_blocks = S // Q_BLOCK
    topk = min(TOPK_MAX, S // 4)
    b_idx = jnp.arange(B)[:, None, None]
    key_pos = jnp.arange(S)

    def to_blocks(t):
        return jnp.swapaxes(t.reshape((B, n_blocks, Q_BLOCK) + t.shape[2:]), 0, 1)

    def block_fn(args):
        qb, iqb, iwb, start = args
        t = start + jnp.arange(Q_BLOCK)
        sc_idx = jnp.einsum('bqhd,bsd->bqhs', iqb, ik).astype(jnp.float32)
        index_score = jnp.einsum('bqhs,bqh->bqs', jax.nn.relu(sc_idx), iwb.astype(jnp.float32))
        admissible = key_pos[None, None, :] <= t[None, :, None]
        index_score = jnp.where(admissible, index_score, -jnp.inf)
        _, sel = lax.top_k(index_score, topk)
        valid = sel <= t[None, :, None]
        k_sel = k[b_idx, sel]
        v_sel = latent[b_idx, sel]
        s = jnp.einsum('bqhd,bqkd->bqhk', qb, k_sel).astype(jnp.float32) * (D ** -0.5)
        s = jnp.where(valid[:, :, None, :], s, -jnp.inf)
        p = jax.nn.softmax(s, axis=-1).astype(v_sel.dtype)
        return jnp.einsum('bqhk,bqkc->bqhc', p, v_sel)

    starts = jnp.arange(n_blocks, dtype=jnp.int32) * Q_BLOCK
    out = lax.map(block_fn, (to_blocks(q), to_blocks(iq), to_blocks(iw), starts))
    return jnp.swapaxes(out, 0, 1).reshape(B, S, HB, latent.shape[-1])

def setup_inputs(seed: int = 0) -> dict:
    key = jax.random.key(seed)
    ks = jax.random.split(key, 12)
    x = jax.random.normal(ks[0], (BATCH, SEQ, D_MODEL), jnp.float32)
    start = jax.random.randint(ks[1], (BATCH, 1), 0, 4096, dtype=jnp.int32)
    positions = (start + jnp.arange(SEQ, dtype=jnp.int32)[None, :]).astype(jnp.int32)

    def gain(k, n):
        return 1.0 + 0.01 * jax.random.normal(k, (DEPTH, n), jnp.float32)

    return {
        "x": x,
        "positions": positions,
        "norm_in_gain": gain(ks[2], D_MODEL),
        "w_in": jax.random.normal(ks[3], (DEPTH, D_MODEL, D_IN), jnp.float32) * D_MODEL ** -0.5,
        "kv_norm_gain": gain(ks[4], KV_LATENT),
        "w_uk": jax.random.normal(ks[5], (DEPTH, KV_LATENT, HEAD_DIM), jnp.float32) * KV_LATENT ** -0.5,
        "w_uv": jax.random.normal(ks[6], (DEPTH, N_HEADS_B, KV_LATENT, HEAD_DIM), jnp.float32) * KV_LATENT ** -0.5,
        "idx_k_norm_gain": gain(ks[7], IDX_DIM),
        "branch_norm_gain_a": gain(ks[8], WIDTH_A),
        "branch_norm_gain_b": gain(ks[9], WIDTH_B),
        "w_out": jax.random.normal(ks[10], (DEPTH, D_MIX, D_MODEL), jnp.float32) * D_MIX ** -0.5,
        "final_norm_gain": 1.0 + 0.01 * jax.random.normal(ks[11], (D_MODEL,), jnp.float32),
    }

def reference(x, positions, norm_in_gain, w_in, kv_norm_gain, w_uk, w_uv, idx_k_norm_gain,
              branch_norm_gain_a, branch_norm_gain_b, w_out, final_norm_gain):
    B, S, _ = x.shape
    cos, sin = rope_tables(positions)
    cos_h, sin_h = cos[:, :, None, :], sin[:, :, None, :]
    h = x
    for layer in range(DEPTH):
        u = rmsnorm(h, norm_in_gain[layer])
        proj = u @ w_in[layer]
        qa, ka, va, za, qb, ckv, zb, iq, ik, iw = split_columns(proj)

        qa = apply_rope(qa.reshape(B, S, N_HEADS_A, HEAD_DIM), cos_h, sin_h)
        ka = apply_rope(ka.reshape(B, S, N_HEADS_A, HEAD_DIM), cos_h, sin_h)
        va = va.reshape(B, S, N_HEADS_A, HEAD_DIM)
        o_a = dilated_mixture(qa, ka, va).reshape(B, S, WIDTH_A)
        y_a = rmsnorm(o_a * jax.nn.silu(za), branch_norm_gain_a[layer])

        qb = apply_rope(qb.reshape(B, S, N_HEADS_B, HEAD_DIM), cos_h, sin_h)
        ckv = rmsnorm(ckv, kv_norm_gain[layer])
        kb = apply_rope(ckv @ w_uk[layer], cos, sin)
        iq = apply_rope(iq.reshape(B, S, IDX_HEADS, IDX_DIM), cos_h, sin_h)
        ik = apply_rope(rmsnorm(ik, idx_k_norm_gain[layer]), cos, sin)
        iw = iw * (IDX_HEADS ** -0.5 * IDX_DIM ** -0.5)
        o_lat = indexed_sparse_attention(qb, kb, ckv, iq, ik, iw)
        o_b = jnp.einsum('bshc,hcd->bshd', o_lat, w_uv[layer]).reshape(B, S, WIDTH_B)
        y_b = rmsnorm(o_b * jax.nn.silu(zb), branch_norm_gain_b[layer])

        h = h + jnp.concatenate([y_a, y_b], axis=-1) @ w_out[layer]
    return rmsnorm(h, final_norm_gain)


_drawn_inputs = setup_inputs


def setup_inputs(seed=0):
    import zlib

    import numpy as np

    out = dict(_drawn_inputs(seed))
    spreads = {}
    factors = {'kv_norm_gain': 19.118,
     'branch_norm_gain_a': 64.0,
     'branch_norm_gain_b': 64.0,
     'final_norm_gain': 31.992}
    for name, (base, spread) in spreads.items():
        noise = np.random.default_rng([zlib.crc32(name.encode()), seed]).standard_normal(out[name].shape)
        drawn = base * np.exp(spread * noise) if base else spread * noise
        out[name] = __import__('jax').numpy.asarray(drawn.astype(out[name].dtype))
    for name, factor in factors.items():
        out[name] = (out[name] * factor).astype(out[name].dtype)
    return out
```

```python
import math

import numpy as np

import concourse.bass as bass
from concourse import mybir
from contextlib import ExitStack

F32 = mybir.dt.float32
F32R = mybir.dt.float32r
I32 = mybir.dt.int32
U8 = mybir.dt.uint8
ALU = mybir.AluOpType
ACT = mybir.ActivationFunctionType

P = 128
SEQ = 1024
D = 1024
HD = 64
HA = HB = 8
WIDTH = HA * HD
ROT, HALF = HD // 4, HD // 8
IH = 4
LAT = 128
TOPK = min(256, SEQ // 4)
EPS = 1e-6
THETA = 500000.0
PATTERNS = ((128, 1), (512, 4), (2048, 16))
SPLITS = (WIDTH, WIDTH, WIDTH, WIDTH, WIDTH, LAT, WIDTH, IH * HD, HD, IH)
OFF = [0]
for _w in SPLITS:
    OFF.append(OFF[-1] + _w)
QA0, KA0, VA0, ZA0, QB0, CKV0, ZB0, IQ0, IK0, IW0, D_IN = OFF
T = SEQ // P
KT = D // P
SCALE = HD ** -0.5
BIG = 1e30
FILL = -3e38

IDXW = IH * HD + HD + IH + LAT
CH_IDX, CH_QA, CH_KA, CH_VA, CH_QB, CH_ZA, CH_ZB, CH_OUT0, CH_OUT1 = range(9)
NIN = 7
CHUNK_COL = {CH_QA: QA0, CH_KA: KA0, CH_VA: VA0, CH_QB: QB0, CH_ZA: ZA0, CH_ZB: ZB0}
CHUNK_W = [IDXW] + [512] * 8
CI_IQ, CI_IK, CI_IW, CI_CKV = 0, IH * HD, IH * HD + HD, IH * HD + HD + IH
NSTAGE = 3
SPILL = 4

SEL = range(TOPK // P, T)
NSEL = len(SEL)
SOFF = {}
_o = 0
for _t in SEL:
    SOFF[_t] = _o
    _o += (_t + 1) * P
STOT = _o
IDX_GROUPS = [(t, k0, min(512, (t + 1) * P - k0)) for t in SEL for k0 in range(0, (t + 1) * P, 512)]

TORD = (7, 0, 6, 1, 5, 2, 4, 3)
HEADS = HA + HB
UNITS = [(head, t) for head in range(HEADS) for t in TORD]
NU = len(UNITS)
PT_PARTS = [[(b, min(4, t + 1 - b)) for b in range(0, t + 1, 4)] for _, t in UNITS]


def prep_names(head):
    return [("q", head, g) for g in range(2)] + [("k", head, g) for g in range(2) if head < HA]


def side_uses(i):
    if i >= NU:
        return []
    head, j = divmod(i, T)
    names = []
    if head == 0 and j < 2:
        names.append(("kbt", j))
    if head + 1 < HEADS and 2 <= j < 2 + len(prep_names(head + 1)):
        names.append(prep_names(head + 1)[j - 2])
    if head < HA and j == 6:
        names.append(("vb", head))
    return names


IDX_STEPS = {(CH_QA, 1): [("ckv", 0), ("ik", 0), ("ckv", 1), ("ik", 1), ("iq", SEL[0])]}
_at = [(CH_QA, 2), (CH_QA, 3)] + [(CH_KA, p) for p in range(4)]
for _n, _t in enumerate(SEL):
    IDX_STEPS[_at[_n]] = ([("iq", _t + 1)] if _t + 1 in SEL else []) + [("score", _t)]


def transpose_uses():
    uses = []
    for t in range(T):
        uses += [(("x", t, g), "V") for g in range(2)]
        if t == 0:
            uses.append((("pos",), "V"))
    for key in sorted(IDX_STEPS):
        uses += [(n, "A" if n[0] == "ckv" else "V") for n in IDX_STEPS[key] if n[0] != "score"]
    uses.append((("kb",), "A"))
    uses += [(n, "V") for n in prep_names(0)]
    for i in range(NU + 3):
        uses += [(n, "A" if n[0] == "vb" else "V") for n in side_uses(i)]
        if 2 <= i < NU + 2:
            uses += [(("p", i - 2, n), "AV"[(i + n) % 2]) for n in range(len(PT_PARTS[i - 2]))]
    for t in range(T):
        uses += [(("y", t, g), "V") for g in range(2)]
    return uses


USES = transpose_uses()
USE_AT = {name: n for n, (name, _) in enumerate(USES)}


def freed(n):
    return sum(e == "A" for _, e in USES[:n + 1]), sum(e == "V" for _, e in USES[:n + 1])


def rounded(n):
    return sum(e == "V" and name[0] not in ("p", "pos") for name, e in USES[:n + 1])


def hybrid_layer(nc, x, positions, norm_in_gain, w_in, kv_norm_gain, w_uk, w_uv, idx_k_norm_gain,
                 branch_norm_gain_a, branch_norm_gain_b, w_out, final_norm_gain, out):
    ctx = ExitStack()
    base = (nc.sbuf_base + 63) // 64 * 64
    limit = nc.sbuf_usable_end
    K = 1024

    def at(name, shape, dt, offset):
        size = int(np.prod(shape[1:])) * mybir.dt.size(dt)
        assert base + offset + size <= limit, (name, base + offset + size, limit)
        return nc.alloc_sbuf_tensor_at(name, shape, dt, offset=base + offset)

    cursor = [0]

    def sb(name, shape, dt=F32):
        o = cursor[0]
        cursor[0] += (int(np.prod(shape[1:])) * mybir.dt.size(dt) + 31) // 32 * 32
        return at(name, shape, dt, o)

    def sem(name):
        return ctx.enter_context(nc.semaphore(name))

    with ctx:
        ident = sb("ident", [P, P])
        strip = sb("strip", [P, SEQ])
        causal = sb("causal", [P, TOPK])
        uk = sb("uk", [P, HD])
        uv = sb("uv", [P, HB, HD])
        g_kv = sb("g_kv", [P, LAT])
        g_ik = sb("g_ik", [P, HD])
        cosd = sb("cosd", [P, T, 2, HALF])
        sind = sb("sind", [P, T, 2, HALF])
        neg_half = sb("neg_half", [P, 2 * T])
        ms = sb("ms", [P, T])
        rs = sb("rs", [P, T])
        ms_i = sb("ms_i", [P, 2 * T])
        rs_i = sb("rs_i", [P, 2 * T])
        ms_y = sb("ms_y", [P, 2 * T])
        rs_y = sb("rs_y", [P, 2 * T])
        ms_o = sb("ms_o", [P, T])
        rs_o = sb("rs_o", [P, T])
        iw = sb("iw", [P, T, IH])
        shift = sb("shift", [P, NU])
        denom = sb("denom", [P, HEADS, T])
        rden = sb("rden", [P, HEADS, T])
        cnt = sb("cnt", [P, NSEL])
        neg = sb("neg", [P, NSEL])
        negi = sb("negi", [P, NSEL], I32)
        sgn = sb("sgn", [P, NSEL], I32)
        acc = sb("acc", [P, NSEL], I32)
        mag = sb("mag", [P, NSEL], I32)
        cand = sb("cand", [P, NSEL], I32)
        bit = sb("bit", [P, 2], I32)
        need = sb("need", [P, NSEL])
        ropeA = sb("ropeA", [P, HA, ROT])
        ropeB = sb("ropeB", [P, HA, ROT])
        o = (cursor[0] + 63) // 64 * 64
        whi = at("whi", [P, KT, 512], F32R, o)
        wlo = at("wlo", [P, KT, 512], F32R, o + 16 * K)
        wraw = at("wraw", [P, NSTAGE, 512], F32, o + 32 * K)
        R = o + (32 + 2 * NSTAGE) * K
        uhi = at("uhi", [P, KT, SEQ], F32R, R)
        ulo = at("ulo", [P, KT, SEQ], F32R, R + 32 * K)
        vb = at("vb", [P, T, WIDTH], F32, R)
        khi = at("khi", [P, 2, SEQ], F32R, R + 16 * K)
        klo = at("klo", [P, 2, SEQ], F32R, R + 24 * K)
        qst = at("qst", [P, 2, SEQ], F32R, R + 32 * K)
        kbhi = at("kbhi", [P, SEQ], F32R, R + 40 * K)
        kblo = at("kblo", [P, SEQ], F32R, R + 44 * K)
        sm = at("sm", [P, 3, SEQ], F32, R + 48 * K)
        kb = at("kb", [P, T, 2, HD], F32, R + 60 * K)
        Q = R + 64 * K
        xraw = at("xraw", [P, T, D], F32, Q)
        qa = at("qa", [P, T, WIDTH], F32, Q)
        ka = at("ka", [P, T, WIDTH], F32, Q + 16 * K)
        qb = at("qb", [P, T, WIDTH], F32, Q + 16 * K)
        sq = at("sq", [P, 2, D], F32, Q)
        S = Q + 32 * K
        score = at("score", [P, STOT], F32, S)
        ckvT = at("ckvT", [P, SEQ], F32, S + 17 * K)
        gin = at("gin", [P, D], F32, S + 17 * K)
        dist = at("dist", [P, SEQ], I32, S)
        resid = at("resid", [P, SEQ], I32, S + 4 * K)
        ikdup = at("ikdup", [P, T, 2, HD], F32, S)
        hit = at("hit", [P, SEQ], F32, S + 8 * K)
        mult = at("mult", [P, SEQ], F32, S + 12 * K)
        hres = at("hres", [P, T, D], F32, S)
        V = S + 21 * K
        proji = at("proji", [P, T, IDXW], F32, V)
        va = at("va", [P, T, WIDTH], F32, V)
        ikhi = at("ikhi", [P, SEQ], F32R, V + 16 * K)
        iklo = at("iklo", [P, SEQ], F32R, V + 20 * K)
        eq = at("eq", [P, SEQ], F32, V + 16 * K)
        rank = at("rank", [P, SEQ], F32, V + 20 * K)
        pt = at("pt", [P, 2, SEQ], F32, V + 16 * K)
        fgain = at("fgain", [P, D], F32, V + 16 * K)
        gy = at("gy", [P, D], F32, V + 20 * K)
        W = V + 24 * K
        iqst = at("iqst", [P, 2, IH * P], F32R, W)
        posr = at("posr", [T, P], I32, W)
        posf = at("posf", [T, P], F32, W + 512)
        ang = at("ang", [P, T, HALF], F32, W + K)
        ang2 = at("ang2", [P, T, HALF], F32, W + K + 256)
        turns = at("turns", [P, T, HALF], F32, W + K + 512)
        turni = at("turni", [P, T, HALF], I32, W + K + 768)
        post = at("post", [P, T], F32, W + 2 * K)
        freq = at("freq", [P, HALF], F32, W + 2 * K + 64)
        hits = at("hits", [P, STOT], U8, W)
        relu = at("relu", [P, 4, 512], F32, W + 4352)
        spill = at("spill", [P, SPILL, 512], F32, W + 4352)
        zin = at("zin", [P, 2, 2, 512], F32, W + 4352)
        kdup = at("kdup", [P, 2, T, 2, HD], F32, W + 4352)
        xsq = at("xsq", [P, 2, D], F32, W + 4352)

        psum = ctx.enter_context(nc.psum_tensor("psum", [P, 8, 512], F32))
        PROJ_BANKS = ((0, 7), (4, 5))
        TBANK = (1, 6)
        OBANK = (0, 7)

        q_dram = nc.dram_tensor("qb_spill", [T, P, WIDTH], F32, kind="Internal").ap()
        z_dram = [nc.dram_tensor(f"z{b}_spill", [T, P, WIDTH], F32, kind="Internal").ap() for b in range(2)]

        s_x = [sem(f"x_in{t}") for t in range(T)]
        s_gin = sem("gin_in")
        s_pos = sem("pos_in")
        s_small = sem("small_in")
        s_w = [sem(f"w_in{n}") for n in range(NSTAGE)]
        s_whi = sem("w_rounded")
        s_wsplit = sem("w_split")
        s_wused = sem("w_used")
        s_const = sem("constants")
        s_ss = sem("x_squares")
        s_mean = sem("x_means")
        s_rs = sem("x_rstd")
        s_xs = sem("x_scaled")
        s_tr = sem("transposed")
        s_hi = sem("rounded_part")
        s_fa = sem("freed_by_act")
        s_fv = sem("freed_by_dve")
        s_proj = sem("projected")
        s_pev = sem("projection_out")
        s_rope = sem("roped")
        s_ropei = sem("rope_step")
        s_posf = sem("pos_float")
        s_ang = sem("angles")
        s_sin = sem("sines")
        s_v = sem("dve_step")
        s_mi = sem("idx_means")
        s_ri = sem("idx_rstd")
        s_ni = sem("idx_normed")
        s_roi = sem("idx_roped")
        s_ikd = sem("idx_key_doubled")
        s_kd = sem("key_doubled")
        s_isc = sem("idx_scores")
        s_rel = sem("idx_relu")
        s_isum = sem("idx_summed")
        s_ifill = sem("idx_causal")
        s_tk = sem("topk_step")
        s_spill = [sem(f"spilled{n}") for n in range(SPILL)]
        s_qb = sem("qb_in")
        s_kbr = sem("kb_roped")
        s_sc = sem("scores")
        s_mk = sem("masked")
        s_ex = sem("exps")
        s_pv = sem("pv")
        s_rd = sem("rden_done")
        s_on = sem("o_normed")
        s_z = [sem(f"z_in{n}") for n in range(2)]
        s_y = sem("gated")
        s_yss = sem("y_squares")
        s_ym = sem("y_means")
        s_yr = sem("y_rstd")
        s_ys = sem("y_scaled")
        s_xr = [sem(f"residual_in{n}") for n in range(4)]
        s_gend = sem("end_gains_in")
        s_h = sem("residual_added")
        s_hs = sem("h_squares")
        s_hm = sem("h_means")
        s_hr = sem("h_rstd")
        s_res = sem("result")
        s_out = sem("stored")

        block = ctx.enter_context(nc.Block())

        def w_count(g):
            return 16 * sum((2 if n < KT else 1) for n in range(g % NSTAGE, g + 1, NSTAGE))

        def tbank(name, lanes=slice(0, P)):
            return psum[lanes, TBANK[USE_AT[name] % 2], :]

        def mask_of(head, t):
            n = (t + 1) * P
            if head < HA:
                return strip[:, SEQ - n:SEQ]
            if t in SOFF:
                return score[:, SOFF[t]:SOFF[t] + n]
            return causal[:, TOPK - n:TOPK]

        def proj_bank(c, t):
            return psum[:, PROJ_BANKS[((c * T + t) // 2) % 2][t % 2], 0:CHUNK_W[c]]

        @block.sync
        def _(sp):
            def load_w(g):
                c, k = divmod(g, KT)
                if g >= NSTAGE:
                    sp.wait_ge(s_wsplit, g - NSTAGE + 1)
                dst, rows, sw = wraw[:, g % NSTAGE, :], slice(k * P, (k + 1) * P), s_w[g % NSTAGE]
                if c == CH_IDX:
                    sp.dma_start(dst[:, 0:CI_CKV], w_in[0, rows, IQ0:D_IN]).then_inc(sw, 16)
                    sp.dma_start(dst[:, CI_CKV:IDXW], w_in[0, rows, CKV0:CKV0 + LAT]).then_inc(sw, 16)
                elif c < NIN:
                    sp.dma_start(dst, w_in[0, rows, CHUNK_COL[c]:CHUNK_COL[c] + 512]).then_inc(sw, 16)
                else:
                    sp.dma_start(dst, w_out[0, rows, (c - NIN) * 512:(c - NIN + 1) * 512]).then_inc(sw, 16)

            sp.dma_start(gin[:, :], norm_in_gain.to_broadcast([P, D])).then_inc(s_gin, 16)
            sp.dma_start(posr[:, :], positions.rearrange("o (t p) -> (o t) p", p=P)).then_inc(s_pos, 16)
            for k in range(KT):
                load_w(k)
            sp.dma_start(g_kv[:, :], kv_norm_gain.to_broadcast([P, LAT])).then_inc(s_small, 16)
            sp.dma_start(g_ik[:, :], idx_k_norm_gain.to_broadcast([P, HD])).then_inc(s_small, 16)
            sp.dma_start(uk[:, :], w_uk[0]).then_inc(s_small, 16)
            sp.dma_start(uv[:, :, :], w_uv[0].rearrange("h c d -> c h d")).then_inc(s_small, 16)

            def store_spill(c, t):
                n = (c - CH_QB) * T + t
                if c == CH_QB:
                    sp.wait_ge(s_rope, 2 * T + t + 1)
                    dst = q_dram
                else:
                    sp.wait_ge(s_pev, c * T + t + 1)
                    dst = z_dram[c - CH_ZA]
                sp.dma_start(dst[t], spill[:, n % SPILL, :]).then_inc(s_spill[n % SPILL], 16)

            for c in range(NIN):
                for k in range(NSTAGE):
                    load_w((c + 1) * KT + k)
                for t in range(6 if c >= CH_QB else 0):
                    store_spill(c, t)
                for k in range(NSTAGE, KT):
                    load_w((c + 1) * KT + k)
                for t in range(6, T if c >= CH_QB else 0):
                    store_spill(c, t)
            for n in range(SPILL):
                sp.wait_ge(s_spill[n], 16 * 3 * T // SPILL)
            sp.wait_ge(s_tr, USE_AT[("k", HA - 1, 1)] + 1)
            sp.dma_start(qb[:, :, :], q_dram.rearrange("t p n -> p t n")).then_inc(s_qb, 16)

            def load_z(t):
                if t >= 2:
                    sp.wait_ge(s_yss, 2 * (t - 1))
                for b in range(2):
                    sp.dma_start(zin[:, t % 2, b, :], z_dram[b][t]).then_inc(s_z[t % 2], 16)

            sp.wait_ge(s_tr, USE_AT[("k", HA - 1, 1)] + 1)
            load_z(0)
            load_z(1)
            sp.wait_ge(s_mk, NU)
            sp.wait_ge(s_pv, NU)
            sp.dma_start(gy[:, 0:WIDTH], branch_norm_gain_a.to_broadcast([P, WIDTH])).then_inc(s_gend, 16)
            sp.dma_start(gy[:, WIDTH:D], branch_norm_gain_b.to_broadcast([P, WIDTH])).then_inc(s_gend, 16)
            sp.dma_start(fgain[:, :], final_norm_gain.unsqueeze(0).to_broadcast([P, D])).then_inc(s_gend, 16)
            xt = x[0].rearrange("(t p) n -> p t n", p=P)
            for t in range(2, T):
                load_z(t)
                if t % 2:
                    n = t // 2 - 1
                    sp.dma_start(hres[:, 2 * n:2 * n + 2, :], xt[:, 2 * n:2 * n + 2, :]).then_inc(s_xr[n], 16)
            sp.dma_start(hres[:, 6:8, :], xt[:, 6:8, :]).then_inc(s_xr[3], 16)
            for k in range(KT):
                load_w(CH_OUT1 * KT + k)
            for t in range(T):
                sp.wait_ge(s_res, t + 1)
                sp.dma_start(out[0, t * P:(t + 1) * P, :], hres[:, t, :]).then_inc(s_out, 16)
            sp.wait_ge(s_out, 16 * T)

        @block.gpsimd
        def _(pool):
            g = nc.gpsimd
            inv = np.float32(THETA) ** (-np.arange(0, ROT, 2, dtype=np.float32) / np.float32(ROT))
            g.memset(ident[:, :], 0.0).then_inc(s_const, 1)
            g.memset(neg_half[:, :], -0.5).then_inc(s_const, 1)
            g.memset(causal[:, :], 0.0).then_inc(s_const, 1)
            for j in range(HALF):
                g.memset(freq[:, j:j + 1], float(inv[j])).then_inc(s_const, 1)
            g.memset(bit[:, 0:1], 1 << 30).then_inc(s_const, 1)
            g.memset(bit[:, 1:2], 30).then_inc(s_const, 1)
            g.memset(mag[:, :], 0).then_inc(s_const, 1)
            zeros_done = 3 + HALF + 3
            pool.wait_ge(s_const, zeros_done)
            g.affine_select(out=ident[:, :], in_=ident[:, :], compare_op=ALU.not_equal, fill=1.0, base=0,
                            pattern=[[-1, P]], channel_multiplier=1).then_inc(s_const, 1)
            g.affine_select(out=causal[:, :], in_=causal[:, :], compare_op=ALU.is_ge, fill=-BIG,
                            base=TOPK - P, pattern=[[-1, TOPK]], channel_multiplier=1).then_inc(s_const, 1)
            g.iota(dist[:, :], pattern=[[-1, SEQ]], base=(T - 1) * P, channel_multiplier=1).then_inc(s_const, 1)

            def w_low(n):
                c, k = divmod(n, KT)
                pool.wait_ge(s_whi, n + 1)
                g.tensor_tensor(wlo[:, k, 0:CHUNK_W[c]], wraw[:, n % NSTAGE, 0:CHUNK_W[c]],
                                whi[:, k, 0:CHUNK_W[c]].bitcast(F32), ALU.subtract).then_inc(s_wsplit, 1)

            def lows(c):
                for k in range(KT):
                    w_low(c * KT + k)

            def rstd(dst, src):
                return g.tensor_tensor(dst, src, neg_half[:, 0:src.shape[1]], ALU.pow)

            steps = [0]

            def rope(v, t, heads, done):
                shape = [P, heads, ROT]
                c = cosd[:, t, :, :].rearrange("p a b -> p (a b)").unsqueeze(1).to_broadcast(shape)
                s = sind[:, t, :, :].rearrange("p a b -> p (a b)").unsqueeze(1).to_broadcast(shape)
                g.tensor_tensor(ropeA[:, 0:heads, :], v[:, :, 0:ROT], c, ALU.mult).then_inc(s_ropei, 1)
                g.tensor_tensor(ropeB[:, 0:heads, :], v[:, :, 0:ROT], s, ALU.mult).then_inc(s_ropei, 1)
                pool.wait_ge(s_ropei, steps[0] + 2)
                g.tensor_tensor(v[:, :, 0:HALF], ropeA[:, 0:heads, 0:HALF], ropeB[:, 0:heads, HALF:ROT],
                                ALU.subtract).then_inc(s_ropei, 1)
                g.tensor_tensor(v[:, :, HALF:ROT], ropeA[:, 0:heads, HALF:ROT], ropeB[:, 0:heads, 0:HALF],
                                ALU.add).then_inc(done[0], 1)
                steps[0] += 3
                done[1] += 1
                pool.wait_ge(s_ropei, steps[0])
                pool.wait_ge(done[0], done[1])

            for t in range(T):
                pool.wait_ge(s_mean, t + 1)
                rstd(rs[:, t:t + 1], ms[:, t:t + 1]).then_inc(s_rs, 1)
                for k in range(2 * t, min(2 * t + 2, KT)):
                    w_low(k)

            def double(head):
                if head == 0:
                    for n in range(SPILL):
                        pool.wait_ge(s_spill[n], 16 * 3 * T // SPILL)
                if head >= 2:
                    pool.wait_ge(s_tr, USE_AT[("k", head - 2, 1)] + 1)
                src = ka[:, :, head * HD:(head + 1) * HD].unsqueeze(2).to_broadcast([P, T, 2, HD])
                g.tensor_copy(kdup[:, head % 2], src).then_inc(s_kd, 1)

            roped, roped_i, roped_kb = [s_rope, 0], [s_roi, 0], [s_kbr, 0]

            def rope_tile(c, t):
                pool.wait_ge(s_pev, c * T + t + 1)
                v = {CH_QA: qa[:, t, :], CH_KA: ka[:, t, :], CH_QB: spill[:, t % SPILL, :]}[c]
                rope(v.rearrange("p (h d) -> p h d", d=HD), t, HA, roped)

            lows(CH_QA)
            pool.wait_ge(s_sin, 4)
            pool.wait_ge(s_mi, 1)
            rstd(rs_i[:, :], ms_i[:, :]).then_inc(s_ri, 1)
            for t in range(T):
                pool.wait_ge(s_ni, t + 1)
                rope(proji[:, t, 0:CI_IW].rearrange("p (h d) -> p h d", d=HD), t, IH + 1, roped_i)
            for c in range(CH_QA, NIN):
                turned = c in (CH_QA, CH_KA, CH_QB)
                for t in range(6 if turned else 0):
                    rope_tile(c, t)
                lows(c + 1)
                for t in range(6, T if turned else 0):
                    rope_tile(c, t)
                if c == CH_KA:
                    for t in SEL:
                        last = max(i for i, grp in enumerate(IDX_GROUPS) if grp[0] == t)
                        pool.wait_ge(s_isum, IH * (last + 1))
                        d = score[:, SOFF[t] + t * P:SOFF[t] + (t + 1) * P]
                        g.affine_select(out=d, in_=d, compare_op=ALU.is_ge, fill=FILL, base=0,
                                        pattern=[[-1, P]], channel_multiplier=1).then_inc(s_ifill, 1)
            pool.wait_ge(s_fa, freed(USE_AT[("kb",)])[0])
            for t in range(T):
                rope(kb[:, t, :, :], t, 2, roped_kb)
                if t < 2:
                    double(t)
            for head in range(2, HA):
                double(head)
            for t in range(T):
                pool.wait_ge(s_ym, t + 1)
                rstd(rs_y[:, 2 * t:2 * t + 2], ms_y[:, 2 * t:2 * t + 2]).then_inc(s_yr, 1)
            lows(CH_OUT1)
            for t in range(T):
                pool.wait_ge(s_hm, t + 1)
                rstd(rs_o[:, t:t + 1], ms_o[:, t:t + 1]).then_inc(s_hr, 1)

        @block.scalar
        def _(act):
            a = nc.scalar

            def w_high(n):
                c, k = divmod(n, KT)
                act.wait_ge(s_w[n % NSTAGE], w_count(n))
                if c:
                    if k < KT - 1:
                        act.wait_ge(s_wused, (c - 1) * (KT - 1) + k + 1)
                    else:
                        act.wait_ge(s_proj, c * T)
                a.activation(whi[:, k, 0:CHUNK_W[c]], wraw[:, n % NSTAGE, 0:CHUNK_W[c]], ACT.Copy)\
                    .then_inc(s_whi, 1)

            def highs(c):
                for k in range(KT):
                    w_high(c * KT + k)

            def part_high(name, dst):
                act.wait_ge(s_tr, USE_AT[name] + 1)
                a.activation(dst, tbank(name, slice(0, dst.shape[0])), ACT.Copy).then_inc(s_hi, 1)

            def bank_copy(name, dst):
                act.wait_ge(s_tr, USE_AT[name] + 1)
                a.activation(dst, tbank(name)[:, 0:dst.free_size()], ACT.Copy).then_inc(s_fa, 1)

            def squares(t):
                act.wait_ge(s_x[t], 16)
                if t >= 2:
                    act.wait_ge(s_ss, t - 1)
                a.activation(xsq[:, t % 2, :], xraw[:, t, :], ACT.Square, accum_out=ms[:, t:t + 1])\
                    .then_inc(s_ss, 1)

            for t in range(T):
                act.dma_start(xraw[:, t, :], x[0, t * P:(t + 1) * P, :]).then_inc(s_x[t], 16)
            squares(0)
            squares(1)
            for t in range(T):
                for k in range(2 * t, min(2 * t + 2, KT)):
                    w_high(k)
                if t == 1:
                    act.wait_ge(s_ang, 1)
                    for j in range(2):
                        a.activation(sind[:, :, j, :], ang[:, :, :], ACT.Sin).then_inc(s_sin, 1)
                        a.activation(cosd[:, :, j, :], ang2[:, :, :], ACT.Sin).then_inc(s_sin, 1)
                for gg in range(2):
                    part_high(("x", t, gg), uhi[:, 4 * gg:4 * gg + 4, t * P:(t + 1) * P])
                if t + 2 < T:
                    squares(t + 2)

            def evac(c, t):
                act.wait_ge(s_proj, c * T + t + 1)
                fn, n = ACT.Copy, (c - CH_QB) * T + t
                if c == CH_IDX:
                    dst = proji[:, t, :]
                elif c in (CH_QA, CH_KA):
                    dst = (qa if c == CH_QA else ka)[:, t, :]
                elif c == CH_VA:
                    act.wait_ge(s_isum, IH * len(IDX_GROUPS))
                    dst = va[:, t, :]
                else:
                    if n >= SPILL:
                        act.wait_ge(s_spill[n % SPILL], 16 * (n // SPILL))
                    dst = spill[:, n % SPILL, :]
                    fn = ACT.Copy if c == CH_QB else ACT.Silu
                a.activation(dst, proj_bank(c, t), fn).then_inc(s_pev, 1)

            def idx_step(name):
                if name[0] == "ckv":
                    bank_copy(name, ckvT[:, name[1] * 512:(name[1] + 1) * 512])
                elif name[0] == "ik":
                    part_high(name, ikhi[:, name[1] * 512:(name[1] + 1) * 512])
                elif name[0] == "iq":
                    t = name[1]
                    if t - 2 in SEL:
                        last = max(i for i, grp in enumerate(IDX_GROUPS) if grp[0] == t - 2)
                        act.wait_ge(s_isc, IH * (last + 1))
                    part_high(name, iqst[0:HD, t % 2, :])
                else:
                    for i, (t, k0, w) in enumerate(IDX_GROUPS):
                        if t != name[1]:
                            continue
                        for h in range(IH):
                            n = IH * i + h
                            act.wait_ge(s_isc, n + 1)
                            if n >= 4:
                                act.wait_ge(s_isum, n - 3)
                            a.activation(relu[:, n % 4, 0:w], psum[:, 2 + n % 2, 0:w], ACT.Relu)\
                                .then_inc(s_rel, 1)

            for c in range(NIN):
                for p in range(4):
                    if p == 3:
                        highs(c + 1)
                    evac(c, 2 * p)
                    evac(c, 2 * p + 1)
                    for name in IDX_STEPS.get((c, p), ()):
                        idx_step(name)

            def side(name):
                kind, head = name[0], name[1]
                if kind == "vb":
                    bank_copy(name, vb[:, head, :])
                    return
                if kind == "kbt":
                    part_high(name, kbhi[:, head * 512:(head + 1) * 512])
                    return
                cols = slice(name[2] * 512, (name[2] + 1) * 512)
                if head >= 2:
                    act.wait_ge(s_sc, T * (head - 1))
                part_high(name, qst[0:HD, head % 2, cols] if kind == "q" else khi[:, head % 2, cols])

            act.wait_ge(s_tr, USE_AT[("kb",)] + 1)
            src = tbank(("kb",)).rearrange("p (t d) -> p t d", d=HD).unsqueeze(2).to_broadcast([P, T, 2, HD])
            a.activation(kb[:, :, :, :], src, ACT.Copy).then_inc(s_fa, 1)
            for name in prep_names(0):
                side(name)
            for i in range(NU + 3):
                for name in side_uses(i):
                    side(name)
                if 2 <= i < NU + 2:
                    u = i - 2
                    for n, (b, nb) in enumerate(PT_PARTS[u]):
                        if USES[USE_AT[("p", u, n)]][1] == "A":
                            if u >= 2:
                                act.wait_ge(s_pv, u - 1)
                            bank_copy(("p", u, n), pt[:, u % 2, b * P:(b + nb) * P])
                if i < NU:
                    head, t = UNITS[i]
                    act.wait_ge(s_mk, i + 1)
                    v = sm[:, i % 3, 0:(t + 1) * P]
                    a.activation(v, v, ACT.Exp, bias=shift[:, i:i + 1], scale=-1.0,
                                 accum_out=denom[:, head, t:t + 1]).then_inc(s_ex, 1)

            def y_squares(t):
                for b in range(2):
                    act.wait_ge(s_y, 2 * t + b + 1)
                    y = (qa if b == 0 else qb)[:, t, :]
                    a.activation(zin[:, t % 2, b, :], y, ACT.Square,
                                 accum_out=ms_y[:, 2 * t + b:2 * t + b + 1]).then_inc(s_yss, 1)

            def y_high(t):
                for gg in range(2):
                    part_high(("y", t, gg), uhi[:, 4 * gg:4 * gg + 4, t * P:(t + 1) * P])

            for t in range(T):
                y_squares(t)
                if t >= 3:
                    y_high(t - 3)
            for t in range(T - 3, T):
                y_high(t)
            highs(CH_OUT1)
            for t in range(T):
                act.wait_ge(s_h, T + t + 1)
                if t >= 2:
                    act.wait_ge(s_hs, t - 1)
                a.activation(sq[:, t % 2, :], hres[:, t, :], ACT.Square, accum_out=ms_o[:, t:t + 1])\
                    .then_inc(s_hs, 1)

        @block.tensor
        def _(pe):
            te = nc.tensor

            def bank_free(name):
                n = USE_AT[name]
                if n >= 2:
                    by_act, by_dve = freed(n - 2)
                    if by_act:
                        pe.wait_ge(s_fa, by_act)
                    if by_dve:
                        pe.wait_ge(s_fv, by_dve)

            def turn(name, tiles):
                bank_free(name)
                b = tbank(name)
                for j, v in enumerate(tiles):
                    ins = te.matmul(b[0:v.shape[1], j * P:(j + 1) * P], v, ident[:, :], start=True, stop=True,
                                    is_transpose=True)
                ins.then_inc(s_tr, 1)

            def both(v):
                return v.rearrange("p a d -> p (a d)")

            def x_turn(t):
                pe.wait_ge(s_xs, t + 1)
                for gg in range(2):
                    turn(("x", t, gg), [xraw[:, t, (4 * gg + j) * P:(4 * gg + j + 1) * P] for j in range(4)])

            def pair(c, p, src_ready):
                q = c * 4 + p
                if 2 <= q < NIN * 4:
                    pe.wait_ge(s_pev, 2 * (q - 1))
                if q >= NIN * 4 + 2:
                    pe.wait_ge(s_h, 2 * (q - NIN * 4 - 1))
                w = CHUNK_W[c]
                for k in range(KT):
                    if p == 0:
                        pe.wait_ge(s_wsplit, c * KT + k + 1)
                    for t in (2 * p, 2 * p + 1):
                        dst, cols = proj_bank(c, t), slice(t * P, (t + 1) * P)
                        if k == 0:
                            src_ready(t)
                        te.matmul(dst, uhi[:, k, cols], whi[:, k, 0:w], start=(k == 0), stop=False)
                        te.matmul(dst, uhi[:, k, cols], wlo[:, k, 0:w], start=False, stop=False)
                        ins = te.matmul(dst, ulo[:, k, cols], whi[:, k, 0:w], start=False, stop=(k == KT - 1))
                        if k == KT - 1:
                            ins.then_inc(s_proj, 1)
                        elif p == 3 and t == T - 1:
                            ins.then_inc(s_wused, 1)

            def split_done(name):
                return lambda: pe.wait_ge(s_fv, freed(USE_AT[name])[1])

            def idx_step(name):
                if name[0] == "ckv":
                    pe.wait_ge(s_ni, 4 * (name[1] + 1))
                    turn(name, [proji[:, 4 * name[1] + j, CI_CKV:IDXW] for j in range(4)])
                elif name[0] == "ik":
                    pe.wait_ge(s_ikd, 1)
                    turn(name, [both(ikdup[:, 4 * name[1] + j]) for j in range(4)])
                elif name[0] == "iq":
                    pe.wait_ge(s_roi, name[1] + 1)
                    turn(name, [proji[:, name[1], h * HD:(h + 1) * HD] for h in range(IH)])
                else:
                    pe.wait_ge(s_fv, freed(USE_AT[("iq", name[1])])[1])
                    for i, (t, k0, w) in enumerate(IDX_GROUPS):
                        if t != name[1]:
                            continue
                        for h in range(IH):
                            n = IH * i + h
                            if n >= 2:
                                pe.wait_ge(s_rel, n - 1)
                            dst, q = psum[:, 2 + n % 2, 0:w], iqst[:, t % 2, h * P:(h + 1) * P]
                            te.matmul(dst, q, ikhi[:, k0:k0 + w], start=True, stop=False)
                            te.matmul(dst, q, iklo[:, k0:k0 + w], start=False, stop=True).then_inc(s_isc, 1)

            pe.wait_ge(s_const, 3 + HALF + 3 + 1)
            x_turn(0)
            pe.wait_ge(s_posf, 1)
            bank_free(("pos",))
            te.matmul(tbank(("pos",))[:, 0:T], posf[:, :], ident[0:T, 0:T], start=True, stop=True,
                      is_transpose=True).then_inc(s_tr, 1)
            for t in range(1, 4):
                x_turn(t)
            for c in range(NIN):
                for p in range(4):
                    if c == 0 and p in (1, 2):
                        x_turn(2 * p + 2)
                        x_turn(2 * p + 3)
                    pair(c, p, lambda t: pe.wait_ge(s_fv, freed(USE_AT[("x", t, 1)])[1]) if c == 0 else None)
                    for name in IDX_STEPS.get((c, p), ()):
                        idx_step(name)

            def side(name):
                kind, head = name[0], name[1]
                if kind == "vb":
                    bank_free(name)
                    te.matmul(tbank(name), ckvT[:, head * P:(head + 1) * P],
                              uv[:, :, :].rearrange("p h d -> p (h d)"), start=True, stop=True).then_inc(s_tr, 1)
                elif kind == "kbt":
                    pe.wait_ge(s_kbr, 4 * (head + 1))
                    turn(name, [both(kb[:, 4 * head + j]) for j in range(4)])
                else:
                    if head == HA and kind == "q":
                        pe.wait_ge(s_qb, 16)
                    if kind == "k":
                        pe.wait_ge(s_kd, head + 1)
                        turn(name, [both(kdup[:, head % 2, 4 * name[2] + j]) for j in range(4)])
                        return
                    src = qa if head < HA else qb
                    cols = slice(head % HA * HD, (head % HA + 1) * HD)
                    turn(name, [src[:, 4 * name[2] + j, cols] for j in range(4)])

            def scores(i):
                head, t = UNITS[i]
                n = (t + 1) * P
                if i >= 2:
                    pe.wait_ge(s_mk, i - 1)
                if i % T == 0:
                    pe.wait_ge(s_fv, freed(USE_AT[prep_names(head)[-1]])[1])
                    if head == HA:
                        pe.wait_ge(s_fv, freed(USE_AT[("kbt", 1)])[1])
                q = qst[:, head % 2, t * P:(t + 1) * P]
                for k0 in range(0, n, 512):
                    w = min(512, n - k0)
                    dst = psum[:, 2 + 2 * (i % 2) + k0 // 512, 0:w]
                    hi = (khi[:, head % 2, :] if head < HA else kbhi)[:, k0:k0 + w]
                    lo = (klo[:, head % 2, :] if head < HA else kblo)[:, k0:k0 + w]
                    te.matmul(dst, q, hi, start=True, stop=False)
                    ins = te.matmul(dst, q, lo, start=False, stop=True)
                ins.then_inc(s_sc, 1)

            def p_turn(u):
                pe.wait_ge(s_ex, u + 1)
                for n, (b, nb) in enumerate(PT_PARTS[u]):
                    turn(("p", u, n), [sm[:, u % 3, (b + j) * P:(b + j + 1) * P] for j in range(nb)])

            def values(u):
                head, t = UNITS[u]
                by_act, by_dve = freed(USE_AT[("p", u, len(PT_PARTS[u]) - 1)])
                pe.wait_ge(s_fa, by_act)
                pe.wait_ge(s_fv, by_dve)
                if u % T == 0 and head >= 2:
                    pe.wait_ge(s_on, head - 1)
                v = va if head < HA else vb
                cols = slice(head % HA * HD, (head % HA + 1) * HD)
                dst = psum[:, OBANK[head % 2], t * HD:(t + 1) * HD]
                for b in range(t + 1):
                    ins = te.matmul(dst, pt[:, u % 2, b * P:(b + 1) * P], v[:, b, cols],
                                    start=(b == 0), stop=(b == t))
                ins.then_inc(s_pv, 1)

            pe.wait_ge(s_pev, NIN * T)
            pe.wait_ge(s_rel, IH * len(IDX_GROUPS))
            bank_free(("kb",))
            for t in range(T):
                ins = te.matmul(tbank(("kb",))[:, t * HD:(t + 1) * HD], ckvT[:, t * P:(t + 1) * P], uk[:, :],
                                start=True, stop=True)
            ins.then_inc(s_tr, 1)
            pe.wait_ge(s_rope, 2 * T)
            for name in prep_names(0):
                side(name)
            for i in range(NU + 3):
                for name in side_uses(i):
                    side(name)
                if i < NU:
                    scores(i)
                if 2 <= i < NU + 2:
                    p_turn(i - 2)
                if i >= 3:
                    values(i - 3)

            def y_turn(t):
                pe.wait_ge(s_ys, 2 * t + 2)
                for gg in range(2):
                    y = qa if gg == 0 else qb
                    turn(("y", t, gg), [y[:, t, j * P:(j + 1) * P] for j in range(4)])

            for t in range(4):
                y_turn(t)
            for c in (CH_OUT0, CH_OUT1):
                for p in range(4):
                    if c == CH_OUT0 and p in (1, 2):
                        y_turn(2 * p + 2)
                        y_turn(2 * p + 3)
                    if c == CH_OUT0 and p < 2:
                        pe.wait_ge(s_on, HEADS)
                    pair(c, p, lambda t: pe.wait_ge(s_fv, freed(USE_AT[("y", t, 1)])[1]) if c == CH_OUT0 else None)

        @block.vector
        def _(dve):
            v = nc.vector
            n_steps = [0]

            def step(ins):
                n_steps[0] += 1
                ins.then_inc(s_v, 1)
                dve.wait_ge(s_v, n_steps[0])

            def part_low(name, dst, hi, lanes=slice(0, P)):
                dve.wait_ge(s_hi, rounded(USE_AT[name]))
                v.tensor_tensor(dst, tbank(name, lanes), hi.bitcast(F32), ALU.subtract).then_inc(s_fv, 1)

            dve.wait_ge(s_pos, 16)
            v.tensor_copy(posf[:, :], posr[:, :]).then_inc(s_posf, 1)

            def x_mean(t):
                dve.wait_ge(s_ss, t + 1)
                v.tensor_scalar(ms[:, t:t + 1], ms[:, t:t + 1], 1.0 / D, EPS, ALU.mult, ALU.add)\
                    .then_inc(s_mean, 1)

            def x_scale(t):
                dve.wait_ge(s_rs, t + 1)
                if t == 0:
                    dve.wait_ge(s_gin, 16)
                v.scalar_tensor_tensor(xraw[:, t, :], xraw[:, t, :], rs[:, t:t + 1], gin[:, :],
                                       ALU.mult, ALU.mult).then_inc(s_xs, 1)

            def u_low(kind, t):
                for gg in range(2):
                    cols = slice(t * P, (t + 1) * P)
                    part_low((kind, t, gg), ulo[:, 4 * gg:4 * gg + 4, cols], uhi[:, 4 * gg:4 * gg + 4, cols])

            def angles():
                flat = [P, T * HALF]
                dve.wait_ge(s_tr, USE_AT[("pos",)] + 1)
                v.tensor_copy(post[:, :], tbank(("pos",))[:, 0:T]).then_inc(s_fv, 1)
                dve.wait_ge(s_fv, freed(USE_AT[("pos",)])[1])
                dve.wait_ge(s_const, 3 + HALF)
                step(v.tensor_tensor(ang[:, :, :], post[:, :].unsqueeze(2).to_broadcast([P, T, HALF]),
                                     freq[:, :].unsqueeze(1).to_broadcast([P, T, HALF]), ALU.mult))
                step(v.tensor_scalar(turns[:, :, :], ang[:, :, :], 1.0 / (2 * math.pi), None, ALU.mult))
                step(v.tensor_copy(turni[:, :, :], turns[:, :, :]))
                step(v.tensor_copy(turns[:, :, :], turni[:, :, :]))
                c1 = 6.28125
                c2 = float(np.float32(np.round((2 * math.pi - c1) * 2 ** 20) / 2 ** 20))
                c3 = 2 * math.pi - c1 - c2
                for part in (c1, c2, c3):
                    step(v.scalar_tensor_tensor(ang[:, :, :], turns[:, :, :], -part, ang[:, :, :],
                                                ALU.mult, ALU.add))
                top = float(np.float32(3.1415925))
                step(v.tensor_scalar(ang[:, :, :], ang[:, :, :], top, -top, ALU.min, ALU.max))
                step(v.tensor_scalar(turns[:, :, :], ang[:, :, :], -1.0, None, ALU.mult))
                step(v.tensor_tensor(ang2[:, :, :], ang[:, :, :], turns[:, :, :], ALU.max))
                v.tensor_scalar(ang2[:, :, :], ang2[:, :, :], -1.0, math.pi / 2, ALU.mult, ALU.add)\
                    .then_inc(s_ang, 1)

            x_mean(0)
            x_scale(0)
            x_mean(1)
            x_scale(1)
            for t in range(T):
                u_low("x", t)
                if t == 0:
                    angles()
                if t + 2 < T:
                    x_mean(t + 2)
                    x_scale(t + 2)

            dve.wait_ge(s_const, 3 + HALF + 3 + 3)
            for n, (window, dilation) in enumerate(PATTERNS):
                step(v.tensor_scalar(resid[:, :], dist[:, :], dilation - 1, None, ALU.bitwise_and))
                step(v.tensor_scalar(hit[:, :], resid[:, :], 0.0, None, ALU.is_equal))
                if n == 0:
                    step(v.scalar_tensor_tensor(mult[:, :], dist[:, :], float(window), hit[:, :],
                                                ALU.is_le, ALU.mult))
                else:
                    step(v.scalar_tensor_tensor(hit[:, :], dist[:, :], float(window), hit[:, :],
                                                ALU.is_le, ALU.mult))
                    step(v.tensor_tensor(mult[:, :], mult[:, :], hit[:, :], ALU.add))
            step(v.scalar_tensor_tensor(mult[:, :], dist[:, :], 0.0, mult[:, :], ALU.is_ge, ALU.mult))
            step(v.tensor_scalar(strip[:, :], mult[:, :], 0.0, -BIG, ALU.is_equal, ALU.mult))
            for m in range(2, len(PATTERNS) + 1):
                step(v.tensor_scalar(hit[:, :], mult[:, :], float(m), math.log(m) / SCALE,
                                     ALU.is_equal, ALU.mult))
                step(v.tensor_tensor(strip[:, :], strip[:, :], hit[:, :], ALU.add))

            for t in range(T):
                dve.wait_ge(s_pev, t + 1)
                for j, (c0, c1) in enumerate(((CI_CKV, IDXW), (CI_IK, CI_IW))):
                    col = proji[:, t, c0:c1]
                    step(v.tensor_tensor_reduce(out=hit[:, 0:c1 - c0], in0=col, in1=col, scale=1.0, scalar=0.0,
                                                op0=ALU.mult, op1=ALU.add,
                                                accum_out=ms_i[:, j * T + t:j * T + t + 1]))
            step(v.tensor_scalar(iw[:, :, :], proji[:, :, CI_IW:CI_CKV], IH ** -0.5 * HD ** -0.5, None, ALU.mult))
            step(v.tensor_scalar(ms_i[:, 0:T], ms_i[:, 0:T], 1.0 / LAT, EPS, ALU.mult, ALU.add))
            v.tensor_scalar(ms_i[:, T:2 * T], ms_i[:, T:2 * T], 1.0 / HD, EPS, ALU.mult, ALU.add).then_inc(s_mi, 1)
            dve.wait_ge(s_ri, 1)
            dve.wait_ge(s_small, 64)
            for t in range(T):
                ckv, ik = proji[:, t, CI_CKV:IDXW], proji[:, t, CI_IK:CI_IW]
                v.scalar_tensor_tensor(ckv, ckv, rs_i[:, t:t + 1], g_kv[:, :], ALU.mult, ALU.mult)
                v.scalar_tensor_tensor(ik, ik, rs_i[:, T + t:T + t + 1], g_ik[:, :], ALU.mult, ALU.mult)\
                    .then_inc(s_ni, 1)

            dve.wait_ge(s_roi, T)
            v.tensor_copy(ikdup[:, :, :, :], proji[:, :, CI_IK:CI_IW].unsqueeze(2).to_broadcast([P, T, 2, HD]))\
                .then_inc(s_ikd, 1)

            for key in sorted(IDX_STEPS):
                for name in IDX_STEPS[key]:
                    if name[0] == "ik":
                        cols = slice(name[1] * 512, (name[1] + 1) * 512)
                        part_low(name, iklo[:, cols], ikhi[:, cols])
                    elif name[0] == "iq":
                        q = iqst[:, name[1] % 2, :]
                        part_low(name, q[HD:P], q[0:HD], slice(0, HD))
                    elif name[0] == "score":
                        for i, (t, k0, w) in enumerate(IDX_GROUPS):
                            if t != name[1]:
                                continue
                            dst = score[:, SOFF[t] + k0:SOFF[t] + k0 + w]
                            for h in range(IH):
                                n = IH * i + h
                                dve.wait_ge(s_rel, n + 1)
                                r, wt = relu[:, n % 4, 0:w], iw[:, t, h:h + 1]
                                if h == 0:
                                    v.tensor_scalar(dst, r, wt, None, ALU.mult).then_inc(s_isum, 1)
                                else:
                                    dve.wait_ge(s_isum, n)
                                    v.scalar_tensor_tensor(dst, r, wt, dst, ALU.mult, ALU.add)\
                                        .then_inc(s_isum, 1)

            dve.wait_ge(s_ifill, NSEL)

            def rows(t):
                return slice(SOFF[t], SOFF[t] + (t + 1) * P)

            def count(op, threshold):
                for j, t in enumerate(SEL):
                    ins = v.tensor_scalar(hits[:, rows(t)], score[:, rows(t)], threshold(j), None, op, ALU.add,
                                          accum_out=cnt[:, j:j + 1])
                return ins

            def candf(j):
                return cand[:, j:j + 1].bitcast(F32)

            step(count(ALU.is_ge, lambda j: 0.0))
            step(v.tensor_scalar(neg[:, :], cnt[:, :], float(TOPK), None, ALU.is_lt))
            step(v.tensor_scalar(negi[:, :], cnt[:, :], float(TOPK), None, ALU.is_lt))
            step(v.tensor_scalar(sgn[:, :], negi[:, :], 31, None, ALU.logical_shift_left))
            with dve.Fori(0, 31) as it:
                v.scalar_tensor_tensor(cand[:, :], mag[:, :], bit[:, 0:1], sgn[:, :],
                                       ALU.bitwise_or, ALU.bitwise_or).then_inc(s_tk, 1)
                dve.wait_ge(s_tk, it * 4 + 1)
                count(ALU.is_ge, candf).then_inc(s_tk, 1)
                dve.wait_ge(s_tk, it * 4 + 2)
                v.scalar_tensor_tensor(acc[:, :], cnt[:, :], float(TOPK), neg[:, :],
                                       ALU.is_ge, ALU.not_equal).then_inc(s_tk, 1)
                dve.wait_ge(s_tk, it * 4 + 3)
                v.scalar_tensor_tensor(mag[:, :], acc[:, :], bit[:, 1:2], mag[:, :],
                                       ALU.logical_shift_left, ALU.bitwise_or)
                v.tensor_scalar(bit[:, 0:1], bit[:, 0:1], 1, None, ALU.logical_shift_right)
                v.tensor_scalar(bit[:, 1:2], bit[:, 1:2], -1.0, None, ALU.add).then_inc(s_tk, 1)
                dve.wait_ge(s_tk, it * 4 + 4)
            step(v.tensor_tensor(mag[:, :], mag[:, :], negi[:, :], ALU.add))
            step(v.tensor_tensor(cand[:, :], mag[:, :], sgn[:, :], ALU.bitwise_or))
            step(count(ALU.is_gt, candf))
            step(v.tensor_scalar(need[:, :], cnt[:, :], -1.0, float(TOPK), ALU.mult, ALU.add))
            for j, t in enumerate(SEL):
                n = (t + 1) * P
                s = score[:, rows(t)]
                step(v.tensor_scalar(eq[:, 0:n], s, candf(j), None, ALU.is_equal))
                step(v.tensor_tensor_scan(rank[:, 0:n], eq[:, 0:n], eq[:, 0:n], 0.0, ALU.add, ALU.max))
                step(v.scalar_tensor_tensor(eq[:, 0:n], rank[:, 0:n], need[:, j:j + 1], eq[:, 0:n],
                                            ALU.is_le, ALU.mult))
                step(v.scalar_tensor_tensor(s, s, candf(j), eq[:, 0:n], ALU.is_gt, ALU.add))
                step(v.tensor_scalar(s, s, BIG, -BIG, ALU.mult, ALU.add))

            def side(name):
                kind, head = name[0], name[1]
                if kind == "vb":
                    return
                if kind == "kbt":
                    cols = slice(head * 512, (head + 1) * 512)
                    part_low(name, kblo[:, cols], kbhi[:, cols])
                    return
                cols = slice(name[2] * 512, (name[2] + 1) * 512)
                if kind == "q":
                    q = qst[:, head % 2, cols]
                    part_low(name, q[HD:P], q[0:HD], slice(0, HD))
                else:
                    part_low(name, klo[:, head % 2, cols], khi[:, head % 2, cols])

            def mask(i):
                head, t = UNITS[i]
                n = (t + 1) * P
                dve.wait_ge(s_sc, i + 1)
                if i >= 3:
                    dve.wait_ge(s_tr, USE_AT[("p", i - 3, len(PT_PARTS[i - 3]) - 1)] + 1)
                b = 2 + 2 * (i % 2)
                src = psum[:, b:b + 2, :].rearrange("p a b -> p (a b)")[:, 0:n]
                v.tensor_tensor_reduce(out=sm[:, i % 3, 0:n], in0=src, in1=mask_of(head, t), scale=-SCALE,
                                       scalar=3e38, op0=ALU.add, op1=ALU.min,
                                       accum_out=shift[:, i:i + 1]).then_inc(s_mk, 1)

            def normalise(head):
                dve.wait_ge(s_pv, T * (head + 1))
                dve.wait_ge(s_ex, T * (head + 1))
                v.reciprocal(rden[:, head, :], denom[:, head, :]).then_inc(s_rd, 1)
                dve.wait_ge(s_rd, head + 1)
                dst = (qa if head < HA else qb)[:, :, head % HA * HD:(head % HA + 1) * HD]
                src = psum[:, OBANK[head % 2], :].rearrange("p (t d) -> p t d", d=HD)
                v.tensor_tensor(dst, src, rden[:, head, :].unsqueeze(2).to_broadcast([P, T, HD]), ALU.mult)\
                    .then_inc(s_on, 1)

            for name in prep_names(0):
                side(name)
            for i in range(NU + 3):
                for name in side_uses(i):
                    side(name)
                if i < NU:
                    mask(i)
                if 2 <= i < NU + 2:
                    u = i - 2
                    for n, (b, nb) in enumerate(PT_PARTS[u]):
                        name = ("p", u, n)
                        if USES[USE_AT[name]][1] == "V":
                            dve.wait_ge(s_tr, USE_AT[name] + 1)
                            if u >= 2:
                                dve.wait_ge(s_pv, u - 1)
                            v.tensor_copy(pt[:, u % 2, b * P:(b + nb) * P], tbank(name)[:, 0:nb * P])\
                                .then_inc(s_fv, 1)
                if i >= T + 3 and (i - 3) % T == 0:
                    normalise((i - 3) // T - 1)
            normalise(HEADS - 1)

            def y_of(b, t):
                return (qa if b == 0 else qb)[:, t, :]

            def gate(t):
                dve.wait_ge(s_z[t % 2], 32 * (t // 2 + 1))
                if t == 0:
                    dve.wait_ge(s_on, HEADS)
                for b in range(2):
                    v.tensor_tensor(y_of(b, t), y_of(b, t), zin[:, t % 2, b, :], ALU.mult).then_inc(s_y, 1)

            def y_mean(t):
                dve.wait_ge(s_yss, 2 * t + 2)
                v.tensor_scalar(ms_y[:, 2 * t:2 * t + 2], ms_y[:, 2 * t:2 * t + 2], 1.0 / WIDTH, EPS,
                                ALU.mult, ALU.add).then_inc(s_ym, 1)

            def y_scale(t):
                dve.wait_ge(s_yr, t + 1)
                if t == 0:
                    dve.wait_ge(s_gend, 48)
                for b in range(2):
                    v.scalar_tensor_tensor(y_of(b, t), y_of(b, t), rs_y[:, 2 * t + b:2 * t + b + 1],
                                           gy[:, b * WIDTH:(b + 1) * WIDTH], ALU.mult, ALU.mult).then_inc(s_ys, 1)

            for t in range(T + 2):
                if t < T:
                    gate(t)
                if 1 <= t <= T:
                    y_mean(t - 1)
                if t >= 2:
                    y_scale(t - 2)
                if 3 <= t < 7:
                    u_low("y", t - 3)

            def residual(c, t):
                half = c - CH_OUT0
                dve.wait_ge(s_proj, c * T + t + 1)
                if half == 0 and t % 2 == 0:
                    dve.wait_ge(s_xr[t // 2], 16)
                d = hres[:, t, half * 512:(half + 1) * 512]
                v.tensor_tensor(d, proj_bank(c, t), d, ALU.add).then_inc(s_h, 1)

            for p in range(4):
                residual(CH_OUT0, 2 * p)
                residual(CH_OUT0, 2 * p + 1)
                if p < 2:
                    u_low("y", 2 * p + 4)
                    u_low("y", 2 * p + 5)

            def h_mean(t):
                dve.wait_ge(s_hs, t + 1)
                v.tensor_scalar(ms_o[:, t:t + 1], ms_o[:, t:t + 1], 1.0 / D, EPS, ALU.mult, ALU.add)\
                    .then_inc(s_hm, 1)

            def result(t):
                dve.wait_ge(s_hr, t + 1)
                v.scalar_tensor_tensor(hres[:, t, :], hres[:, t, :], rs_o[:, t:t + 1], fgain[:, :],
                                       ALU.mult, ALU.mult).then_inc(s_res, 1)

            for p in range(4):
                residual(CH_OUT1, 2 * p)
                residual(CH_OUT1, 2 * p + 1)
                for t in (2 * p, 2 * p + 1):
                    h_mean(t)
                for t in (2 * p, 2 * p + 1):
                    result(t)


_INS = ["x", "positions", "norm_in_gain", "w_in", "kv_norm_gain", "w_uk", "w_uv", "idx_k_norm_gain",
        "branch_norm_gain_a", "branch_norm_gain_b", "w_out", "final_norm_gain"]


def kernel(**inputs):
    import numpy as _np
    import concourse.bacc as _bacc
    from concourse import mybir as _mybir
    from concourse.bass_utils import run_bass_kernel_spmd as _run

    nc = _bacc.Bacc("TRN2", target_bir_lowering=False, num_devices=1)
    arrays, args = {}, []
    for name in _INS:
        a = _np.ascontiguousarray(inputs[name])
        arrays[f"in_{name}"] = a
        args.append(nc.dram_tensor(f"in_{name}", a.shape, _mybir.dt.from_np(a.dtype), kind="ExternalInput").ap())
    args.append(nc.dram_tensor("out", (1, SEQ, D), F32, kind="ExternalOutput").ap())
    hybrid_layer(nc, *args)
    r = _run(nc, [arrays], core_ids=[0])
    return r.results[0]["out"]
```

```python
import math

import numpy as np

import concourse.bass as bass
from concourse import mybir
from contextlib import ExitStack

F32 = mybir.dt.float32
F32R = mybir.dt.float32r
BF16 = mybir.dt.bfloat16
I32 = mybir.dt.int32
U8 = mybir.dt.uint8
ALU = mybir.AluOpType
ACT = mybir.ActivationFunctionType

P = 128
SEQ = 1024
D = 1024
HD = 64
HA = HB = 8
WIDTH = HA * HD
ROT, HALF = HD // 4, HD // 8
IH = 4
LAT = 128
TOPK = min(256, SEQ // 4)
EPS = 1e-6
THETA = 500000.0
PATTERNS = ((128, 1), (512, 4), (2048, 16))
SPLITS = (WIDTH, WIDTH, WIDTH, WIDTH, WIDTH, LAT, WIDTH, IH * HD, HD, IH)
OFF = [0]
for _w in SPLITS:
    OFF.append(OFF[-1] + _w)
QA0, KA0, VA0, ZA0, QB0, CKV0, ZB0, IQ0, IK0, IW0, D_IN = OFF
T = SEQ // P
KT = D // P
SCALE = HD ** -0.5
BIG = 1e30
FILL = -3e38

IDXW = IH * HD + HD + IH + LAT
CH_IDX, CH_QA, CH_KA, CH_VA, CH_QB, CH_ZA, CH_ZB, CH_OUT0, CH_OUT1 = range(9)
NIN = 7
CHUNK_COL = {CH_QA: QA0, CH_KA: KA0, CH_VA: VA0, CH_QB: QB0, CH_ZA: ZA0, CH_ZB: ZB0}
CHUNK_W = [IDXW] + [512] * 8
CI_IQ, CI_IK, CI_IW, CI_CKV = 0, IH * HD, IH * HD + HD, IH * HD + HD + IH
NSTAGE = 3
SPILL = 4

SEL = range(TOPK // P, T)
NSEL = len(SEL)
SOFF = {}
_o = 0
for _t in SEL:
    SOFF[_t] = _o
    _o += (_t + 1) * P
STOT = _o
IDX_GROUPS = [(t, k0, min(512, (t + 1) * P - k0)) for t in SEL for k0 in range(0, (t + 1) * P, 512)]

TORD = (7, 0, 6, 1, 5, 2, 4, 3)
HEADS = HA + HB
UNITS = [(head, t) for head in range(HEADS) for t in TORD]
NU = len(UNITS)
TIE_PARTS = 6
TIE_AT = {3 + 5 * n // 3: n for n in range(TIE_PARTS * NSEL)}
LAG_T, LAG_V = 3, 4
SM_SLOTS, PT_SLOTS = 4, 3
PT_PARTS = [[(b, min(4, t + 1 - b)) for b in range(0, t + 1, 4)] for _, t in UNITS]


def prep_names(head):
    return [("q", head, g) for g in range(2)] + [("k", head, g) for g in range(2) if head < HA]


def side_uses(i):
    if i >= NU:
        return []
    head, j = divmod(i, T)
    names = []
    if head == 0 and j < 2:
        names.append(("kbt", j))
    if head + 1 < HEADS and 2 <= j < 2 + len(prep_names(head + 1)):
        names.append(prep_names(head + 1)[j - 2])
    if head >= HA and j == 6:
        names.append(("ya", head - HA))
    return names


def late_uses(i):
    return [("vb", n) for n in range(3 * i, min(3 * i + 3, T))]


IDX_STEPS = {(CH_QA, 1, 3): [("ckv", 0)], (CH_QA, 1, 4): [("ckv", 1)],
             (CH_QA, 1, 5): [("ik", 0), ("ik", 1)], (CH_QA, 1, 6): [("iq", SEL[0])]}
for _i, (_t, _k0, _w) in enumerate(IDX_GROUPS):
    for _h in range(IH):
        _at = (CH_QA * 4 + 1) * KT + 7 + (IH * _i + _h) // 2
        _names = IDX_STEPS.setdefault((_at // (4 * KT), _at // KT % 4, _at % KT), [])
        if _h == 0 and _k0 == 0 and _t + 1 in SEL:
            _names.append(("iq", _t + 1))
        _names.append(("score", _i, _h))
IDX_STEPS[CH_VA, 0, 3] = [("kb",)]
X_STEPS = {(p, k): 2 * p + 2 + n for p in range(T // 2 - 1) for n, k in enumerate((1, 4) if p else (3, 6))}
IDX_TILES = ((0, T - 4), (T - 4, T - 2), (T - 2, T))


def transpose_uses():
    uses = [(("rows",), "V")]
    for t in range(T):
        uses += [(("x", t, g), "V") for g in range(2)]
        if t == 1:
            uses.append((("gains",), "V"))
    for key in sorted(IDX_STEPS):
        uses += [(n, "A" if n[0] in ("ckv", "kb") else "V") for n in IDX_STEPS[key] if n[0] != "score"]
    uses += [(n, "V") for n in prep_names(0)]
    for i in range(NU + LAG_T):
        uses += [(n, "V") for n in side_uses(i)] + [(n, "A") for n in late_uses(i)]
        if i >= LAG_T:
            u = i - LAG_T
            uses += [(("p", u, n), "A" if part[1] >= 3 else "V") for n, part in enumerate(PT_PARTS[u])]
    uses += [(("yb", t), "V") for t in range(T)]
    return uses


USES = transpose_uses()
USE_AT = {name: n for n, (name, _) in enumerate(USES)}


def bank_ring():
    banks, before, last = [], [], {}
    first, end = USE_AT[("q", 0, 0)], USE_AT[("yb", 0)]
    for n in range(len(USES)):
        ring = (1, 6, 5) if first <= n < end else (1, 6)
        bank = ring[(n - first) % len(ring)]
        banks.append(bank)
        before.append(last.get(bank))
        last[bank] = n
    return banks, before


USE_BANK, USE_BEFORE = bank_ring()


def freed(n):
    return sum(e == "A" for _, e in USES[:n + 1]), sum(e == "V" for _, e in USES[:n + 1])


def rounded(n):
    return sum(e == "V" and name[0] not in ("p", "rows", "gains") for name, e in USES[:n + 1])


def hybrid_layer(nc, x, positions, norm_in_gain, w_in, kv_norm_gain, w_uk, w_uv, idx_k_norm_gain,
                 branch_norm_gain_a, branch_norm_gain_b, w_out, final_norm_gain, out):
    ctx = ExitStack()
    base = (nc.sbuf_base + 63) // 64 * 64
    limit = nc.sbuf_usable_end
    K = 1024

    def at(name, shape, dt, offset):
        size = int(np.prod(shape[1:])) * mybir.dt.size(dt)
        assert base + offset + size <= limit, (name, base + offset + size, limit)
        return nc.alloc_sbuf_tensor_at(name, shape, dt, offset=base + offset)

    cursor = [0]

    def sb(name, shape, dt=F32):
        o = cursor[0]
        cursor[0] += (int(np.prod(shape[1:])) * mybir.dt.size(dt) + 31) // 32 * 32
        return at(name, shape, dt, o)

    def sem(name):
        return ctx.enter_context(nc.semaphore(name))

    with ctx:
        ident = sb("ident", [P, P])
        strip = sb("strip", [P, SEQ])
        causal = sb("causal", [P, TOPK])
        uk = sb("uk", [P, HD])
        uv = sb("uv", [P, HB, HD])
        g_kv = sb("g_kv", [P, LAT])
        g_ik = sb("g_ik", [P, HD])
        cosd = sb("cosd", [P, T, 2, HALF])
        sind = sb("sind", [P, T, 2, HALF])
        neg_half = sb("neg_half", [P, 2 * T])
        ms = sb("ms", [P, T])
        rs = sb("rs", [P, T])
        ms_i = sb("ms_i", [P, 2 * T])
        rs_i = sb("rs_i", [P, 2 * T])
        ms_y = sb("ms_y", [P, 2 * T])
        rs_y = sb("rs_y", [P, 2 * T])
        ms_o = sb("ms_o", [P, 2 * T])
        rs_o = sb("rs_o", [P, T])
        iw = sb("iw", [P, T, IH])
        shift = sb("shift", [P, NU])
        denom = sb("denom", [P, HEADS, T])
        rden = sb("rden", [P, HEADS, T])
        cnt = sb("cnt", [P, NSEL])
        neg = sb("neg", [P, NSEL])
        negi = sb("negi", [P, NSEL], I32)
        sgn = sb("sgn", [P, NSEL], I32)
        acc = sb("acc", [P, NSEL], I32)
        mag = sb("mag", [P, NSEL], I32)
        cand = sb("cand", [P, NSEL], I32)
        bit = sb("bit", [P, 2], I32)
        need = sb("need", [P, NSEL])
        ginT = sb("ginT", [P, KT])
        gyT = sb("gyT", [P, KT])
        ropeA = sb("ropeA", [P, HA, ROT])
        ropeB = sb("ropeB", [P, HA, ROT])
        o = (cursor[0] + 63) // 64 * 64
        whi = at("whi", [P, KT, 512], F32R, o)
        wlo = at("wlo", [P, KT, 512], F32R, o + 16 * K)
        wraw = at("wraw", [P, NSTAGE, 512], F32, o + 32 * K)
        R = o + (32 + 2 * NSTAGE) * K
        uhi = at("uhi", [P, KT, SEQ], F32R, R)
        ulo = at("ulo", [P, KT, SEQ], F32R, R + 32 * K)
        vb = at("vb", [P, T, WIDTH], F32, R)
        khi = at("khi", [P, 2, SEQ], F32R, R + 16 * K)
        klo = at("klo", [P, 2, SEQ], F32R, R + 24 * K)
        qst = at("qst", [P, 2, SEQ], F32R, R + 32 * K)
        kbhi = at("kbhi", [P, SEQ], F32R, R + 40 * K)
        kblo = at("kblo", [P, SEQ], F32R, R + 44 * K)
        sm = at("sm", [P, SM_SLOTS, SEQ], F32, R + 48 * K)
        Q = R + 64 * K
        xraw = at("xraw", [P, T, D], F32, Q)
        qa = at("qa", [P, T, WIDTH], F32, Q)
        ka = at("ka", [P, T, WIDTH], F32, Q + 16 * K)
        qb = at("qb", [P, T, WIDTH], F32, Q + 16 * K)
        S = Q + 32 * K
        score = at("score", [P, STOT], F32, S)
        ckvT = at("ckvT", [P, SEQ], F32, S + 17 * K)
        xsq = at("xsq", [P, 2, D], BF16, S + 17 * K)
        dist = at("dist", [P, SEQ], I32, S)
        resid = at("resid", [P, SEQ], I32, S + 4 * K)
        ikdup = at("ikdup", [P, T, 2, HD], F32, S)
        hit = at("hit", [P, SEQ], F32, S + 8 * K)
        mult = at("mult", [P, SEQ], F32, S + 12 * K)
        hres = [at("hres0", [P, T, 512], F32, S), at("hres1", [P, T, 512], F32, Q)]
        fgain = at("fgain", [P, D], F32, S + 17 * K)
        V = S + 21 * K
        proji = at("proji", [P, T, IDXW], F32, V)
        va = at("va", [P, T, WIDTH], F32, V)
        ikhi = at("ikhi", [P, SEQ], F32R, V + 16 * K)
        iklo = at("iklo", [P, SEQ], F32R, V + 20 * K)
        kdup0 = at("kdup0", [P, T, 2, HD], F32, V + 16 * K)
        kb = at("kb", [P, T, 2, HD], F32, V + 20 * K)
        pt = at("pt", [P, PT_SLOTS, SEQ], F32, V + 16 * K)
        W = V + 24 * K
        iqst = at("iqst", [P, 2, IH * P], F32R, W)
        posr = at("posr", [T, P], I32, W)
        posf = at("posf", [T, P], F32, W + 512)
        ang = at("ang", [P, T, HALF], F32, W + K)
        ang2 = at("ang2", [P, T, HALF], F32, W + K + 256)
        turns = at("turns", [P, T, HALF], F32, W + K + 512)
        turni = at("turni", [P, T, HALF], I32, W + K + 768)
        post = at("post", [P, T], F32, W + 2 * K)
        freq = at("freq", [P, HALF], F32, W + 2 * K + 64)
        junk = at("junk", [P, P], F32, W + 3 * K)
        gyr = at("gyr", [KT, P], F32, W + 2 * K + 640)
        ginr = at("ginr", [KT, P], F32, W + 2 * K + 128)
        eq = at("eq", [P, SEQ], BF16, W + 4352 + 8 * K)
        rank = at("rank", [P, SEQ], F32, o + 32 * K)
        hits = at("hits", [P, STOT], U8, W)
        relu = at("relu", [P, 4, 512], F32, W + 4352)
        spill = at("spill", [P, SPILL, 512], F32, W + 4352)
        za_in = at("za_in", [P, 2, 512], F32, W + 4352)
        zb_in = at("zb_in", [P, 2, T, HD], F32, W + 4352 + 4 * K)
        ysq = at("ysq", [P, 2, 512], BF16, W + 4352 + 8 * K)
        yhi = [at("yhi_a", [P, KT // 2, SEQ], F32R, V), at("yhi_b", [P, KT // 2, SEQ], F32R, R + 32 * K)]
        ylo = [at("ylo_a", [P, KT // 2, SEQ], F32R, R + 16 * K), at("ylo_b", [P, KT // 2, SEQ], F32R, R + 48 * K)]
        whi1 = at("whi1", [P, KT, 512], F32R, R)
        wlo1 = at("wlo1", [P, KT, 512], F32R, V + 16 * K)
        kdup = at("kdup", [P, 2, T, 2, HD], F32, W + 4352)
        wfirst = [at("wfirst0", [P, KT // 2, 512], F32, V + 16 * K),
                  at("wfirst1", [P, KT // 2, 512], F32, W + 4352)]

        psum = ctx.enter_context(nc.psum_tensor("psum", [P, 8, 512], F32))
        PROJ_BANKS = ((0, 7), (4, 5))
        OBANK = (0, 7)
        OUT_BANKS = ((4, 5), (2, 3), (0, 7))

        q_dram = nc.dram_tensor("qb_spill", [T, P, WIDTH], F32, kind="Internal").ap()
        z_dram = [nc.dram_tensor(f"z{b}_spill", [T, P, WIDTH], F32, kind="Internal").ap() for b in range(2)]

        s_x = [sem(f"x_in{t}") for t in range(T)]
        s_gains = sem("branch_gains_in")
        s_rows = sem("gain_and_positions_in")
        s_small = sem("small_in")
        s_wf = [sem(f"w_first{k}_in") for k in range(KT)]
        s_w = [sem(f"w_in{n}") for n in range(NSTAGE)]
        s_wg = sem("w_times_gain")
        s_whi = sem("w_rounded")
        s_wsplit = sem("w_split")
        s_wused = sem("w_used")
        s_const = sem("constants")
        s_ss = sem("x_squares")
        s_mean = sem("x_means")
        s_rs = sem("x_rstd")
        s_tr = sem("transposed")
        s_hi = sem("rounded_part")
        s_fa = sem("freed_by_act")
        s_fv = sem("freed_by_dve")
        s_proj = sem("projected")
        s_pev = sem("projection_out")
        s_rope = sem("roped")
        s_ropei = sem("rope_step")
        s_posf = sem("pos_float")
        s_ang = sem("angles")
        s_sin = sem("sines")
        s_v = sem("dve_step")
        s_mi = sem("idx_means")
        s_ri = sem("idx_rstd")
        s_ni = sem("idx_normed")
        s_roi = sem("idx_roped")
        s_ikd = sem("idx_key_doubled")
        s_kd = sem("key_doubled")
        s_isc = sem("idx_scores")
        s_rel = sem("idx_relu")
        s_isum = sem("idx_summed")
        s_ifill = sem("idx_causal")
        s_tk = sem("topk_step")
        s_spill = [sem(f"spilled{n}") for n in range(SPILL)]
        s_qb = sem("qb_in")
        s_kbr = sem("kb_roped")
        s_sc = sem("scores")
        s_mk = sem("masked")
        s_ex = sem("exps")
        s_pv = sem("pv")
        s_rd = sem("rden_done")
        s_on = sem("o_normed")
        s_za = [sem(f"za_in{n}") for n in range(2)]
        s_zb = [sem(f"zb_in{n}") for n in range(2)]
        s_ya = sem("a_gated")
        s_yb = sem("b_gated")
        s_yss = sem("y_squares")
        s_ym = sem("y_means")
        s_yr = sem("y_rstd")
        s_xr = [[sem(f"residual{c}_in{n}") for n in range(T // 2)] for c in range(2)]
        s_gend = sem("final_gain_in")
        s_h0 = sem("branch_a_added")
        s_h = sem("residual_added")
        s_hs = sem("h_squares")
        s_hm = sem("h_means")
        s_hr = sem("h_rstd")
        s_res = sem("result")
        s_out = sem("stored")

        block = ctx.enter_context(nc.Block())

        def w_landing(n):
            c, k = divmod(n, KT)
            if c == 0:
                return wfirst[k // (KT // 2)][:, k % (KT // 2), 0:IDXW], s_wf[k], 32
            m = n - KT
            return wraw[:, m % NSTAGE, :], s_w[m % NSTAGE], 16 * (m // NSTAGE + 1)

        def tbank(name, lanes=slice(0, P)):
            return psum[lanes, USE_BANK[USE_AT[name]], :]

        def mask_of(head, t):
            n = (t + 1) * P
            if head < HA:
                return strip[:, SEQ - n:SEQ]
            if t in SOFF:
                return score[:, SOFF[t]:SOFF[t] + n]
            return causal[:, TOPK - n:TOPK]

        def w_split(c):
            return (whi1, wlo1) if c == CH_OUT1 else (whi, wlo)

        def proj_bank(c, t):
            return psum[:, PROJ_BANKS[((c * T + t) // 2) % 2][t % 2], 0:CHUNK_W[c]]

        @block.sync
        def _(sp):
            def load_w(g):
                c, k = divmod(g, KT)
                if g >= KT + NSTAGE:
                    sp.wait_ge(s_wsplit, g - NSTAGE + 1)
                dst, sw, _ = w_landing(g)
                rows = slice(k * P, (k + 1) * P)
                if c == CH_IDX:
                    sp.dma_start(dst[:, 0:CI_CKV], w_in[0, rows, IQ0:D_IN]).then_inc(sw, 16)
                    sp.dma_start(dst[:, CI_CKV:IDXW], w_in[0, rows, CKV0:CKV0 + LAT]).then_inc(sw, 16)
                elif c < NIN:
                    sp.dma_start(dst, w_in[0, rows, CHUNK_COL[c]:CHUNK_COL[c] + 512]).then_inc(sw, 16)
                else:
                    sp.dma_start(dst, w_out[0, rows, (c - NIN) * 512:(c - NIN + 1) * 512]).then_inc(sw, 16)

            def x_load(t):
                sp.dma_start(xraw[:, t, :], x[0, t * P:(t + 1) * P, :]).then_inc(s_x[t], 16)

            sp.dma_start(ginr[:, :], norm_in_gain.rearrange("o (t p) -> (o t) p", p=P)).then_inc(s_rows, 16)
            sp.dma_start(posr[:, :], positions.rearrange("o (t p) -> (o t) p", p=P)).then_inc(s_rows, 16)
            for k in range(KT):
                if k in (0, 1, 4, 6):
                    x_load((0, 1, 4, 6).index(k))
                load_w(k)
            for t in range(4, T):
                x_load(t)
            for b, gain in enumerate((branch_norm_gain_a, branch_norm_gain_b)):
                sp.dma_start(gyr[b * KT // 2:(b + 1) * KT // 2, :],
                             gain.rearrange("o (t p) -> (o t) p", p=P)).then_inc(s_gains, 16)
            sp.dma_start(g_kv[:, :], kv_norm_gain.to_broadcast([P, LAT])).then_inc(s_small, 16)
            sp.dma_start(g_ik[:, :], idx_k_norm_gain.to_broadcast([P, HD])).then_inc(s_small, 16)
            sp.dma_start(uk[:, :], w_uk[0]).then_inc(s_small, 16)
            sp.dma_start(uv[:, :, :], w_uv[0].rearrange("h c d -> c h d")).then_inc(s_small, 16)

            def store_spill(c, t):
                n = (c - CH_QB) * T + t
                if c == CH_QB:
                    sp.wait_ge(s_rope, 2 * T + t + 1)
                    dst = q_dram
                else:
                    sp.wait_ge(s_pev, c * T + t + 1)
                    dst = z_dram[c - CH_ZA]
                sp.dma_start(dst[t], spill[:, n % SPILL, :]).then_inc(s_spill[n % SPILL], 16)

            for c in range(NIN):
                for k in range(NSTAGE):
                    load_w((c + 1) * KT + k)
                for t in range(6 if c >= CH_QB else 0):
                    store_spill(c, t)
                for k in range(NSTAGE, KT):
                    load_w((c + 1) * KT + k)
                for t in range(6, T if c >= CH_QB else 0):
                    store_spill(c, t)
            for n in range(SPILL):
                sp.wait_ge(s_spill[n], 16 * 3 * T // SPILL)
            sp.wait_ge(s_tr, USE_AT[("k", HA - 1, 1)] + 1)
            sp.dma_start(qb[:, :, :], q_dram.rearrange("t p n -> p t n")).then_inc(s_qb, 16)

            def load_za(t):
                if t >= 2:
                    sp.wait_ge(s_ya, t - 1)
                sp.dma_start(za_in[:, t % 2, :], z_dram[0][t]).then_inc(s_za[t % 2], 16)

            def load_zb(m):
                if m >= 2:
                    sp.wait_ge(s_yb, m - 1)
                sp.dma_start(zb_in[:, m % 2, :, :], z_dram[1][:, :, m * HD:(m + 1) * HD]
                             .rearrange("t p d -> p t d")).then_inc(s_zb[m % 2], 16)

            for m in range(HB):
                load_za(m)
                load_zb(m)
            for k in range(NSTAGE):
                load_w(CH_OUT1 * KT + k)
            xt = x[0].rearrange("(t p) n -> p t n", p=P)

            def load_residual(c, n):
                sp.dma_start(hres[c][:, 2 * n:2 * n + 2, :], xt[:, 2 * n:2 * n + 2, c * 512:(c + 1) * 512])\
                    .then_inc(s_xr[c][n], 16)

            sp.dma_start(fgain[:, :], final_norm_gain.unsqueeze(0).to_broadcast([P, D])).then_inc(s_gend, 16)
            sp.wait_ge(s_tr, USE_AT[("ya", T - 1)] + 1)
            sp.wait_ge(s_yss, T)
            for n in range(T // 2):
                load_residual(1, n)
            sp.wait_ge(s_mk, NU)
            for n in range(T // 2):
                load_residual(0, n)
            for k in range(NSTAGE, KT):
                load_w(CH_OUT1 * KT + k)
            for t in range(T):
                sp.wait_ge(s_res, 2 * t + 2)
                for c in range(2):
                    sp.dma_start(out[0, t * P:(t + 1) * P, c * 512:(c + 1) * 512], hres[c][:, t, :])\
                        .then_inc(s_out, 16)
            sp.wait_ge(s_out, 32 * T)

        @block.gpsimd
        def _(pool):
            g = nc.gpsimd
            inv = np.float32(THETA) ** (-np.arange(0, ROT, 2, dtype=np.float32) / np.float32(ROT))
            g.memset(ident[:, :], 0.0).then_inc(s_const, 1)
            g.memset(neg_half[:, :], -0.5).then_inc(s_const, 1)
            g.memset(causal[:, :], 0.0).then_inc(s_const, 1)
            for j in range(HALF):
                g.memset(freq[:, j:j + 1], float(inv[j])).then_inc(s_const, 1)
            g.memset(bit[:, 0:1], 1 << 30).then_inc(s_const, 1)
            g.memset(bit[:, 1:2], 30).then_inc(s_const, 1)
            g.memset(mag[:, :], 0).then_inc(s_const, 1)
            zeros_done = 3 + HALF + 3
            pool.wait_ge(s_const, zeros_done)
            g.affine_select(out=ident[:, :], in_=ident[:, :], compare_op=ALU.not_equal, fill=1.0, base=0,
                            pattern=[[-1, P]], channel_multiplier=1).then_inc(s_const, 1)
            g.affine_select(out=causal[:, :], in_=causal[:, :], compare_op=ALU.is_ge, fill=-BIG,
                            base=TOPK - P, pattern=[[-1, TOPK]], channel_multiplier=1).then_inc(s_const, 1)
            g.iota(dist[:, :], pattern=[[-1, SEQ]], base=(T - 1) * P, channel_multiplier=1).then_inc(s_const, 1)

            def w_low(n):
                c, k = divmod(n, KT)
                pool.wait_ge(s_whi, n + 1)
                raw, hi = w_landing(n)[0], w_split(c)[0][:, k, 0:CHUNK_W[c]].bitcast(F32)
                g.tensor_tensor(w_split(c)[1][:, k, 0:CHUNK_W[c]], raw, hi, ALU.subtract).then_inc(s_wsplit, 1)

            def lows(c):
                for k in range(KT):
                    w_low(c * KT + k)

            def rstd(dst, src):
                return g.tensor_tensor(dst, src, neg_half[:, 0:src.shape[1]], ALU.pow)

            steps = [0]

            def rope(v, t, heads, done):
                shape = [P, heads, ROT]
                c = cosd[:, t, :, :].rearrange("p a b -> p (a b)").unsqueeze(1).to_broadcast(shape)
                s = sind[:, t, :, :].rearrange("p a b -> p (a b)").unsqueeze(1).to_broadcast(shape)
                g.tensor_tensor(ropeA[:, 0:heads, :], v[:, :, 0:ROT], c, ALU.mult).then_inc(s_ropei, 1)
                g.tensor_tensor(ropeB[:, 0:heads, :], v[:, :, 0:ROT], s, ALU.mult).then_inc(s_ropei, 1)
                pool.wait_ge(s_ropei, steps[0] + 2)
                g.tensor_tensor(v[:, :, 0:HALF], ropeA[:, 0:heads, 0:HALF], ropeB[:, 0:heads, HALF:ROT],
                                ALU.subtract).then_inc(s_ropei, 1)
                g.tensor_tensor(v[:, :, HALF:ROT], ropeA[:, 0:heads, HALF:ROT], ropeB[:, 0:heads, 0:HALF],
                                ALU.add).then_inc(done[0], 1)
                steps[0] += 3
                done[1] += 1
                pool.wait_ge(s_ropei, steps[0])
                pool.wait_ge(done[0], done[1])

            lows(CH_IDX)
            for t in range(T):
                pool.wait_ge(s_mean, t + 1)
                rstd(rs[:, t:t + 1], ms[:, t:t + 1]).then_inc(s_rs, 1)

            def double(head):
                if head == 1:
                    for n in range(SPILL):
                        pool.wait_ge(s_spill[n], 16 * 3 * T // SPILL)
                if head >= 2:
                    pool.wait_ge(s_tr, USE_AT[("k", head - 2, 1)] + 1)
                src = ka[:, :, head * HD:(head + 1) * HD].unsqueeze(2).to_broadcast([P, T, 2, HD])
                g.tensor_copy(kdup[:, head % 2] if head else kdup0[:, :, :, :], src).then_inc(s_kd, 1)

            roped, roped_i, roped_kb = [s_rope, 0], [s_roi, 0], [s_kbr, 0]

            def rope_tile(c, t):
                pool.wait_ge(s_pev, c * T + t + 1)
                v = {CH_QA: qa[:, t, :], CH_KA: ka[:, t, :], CH_QB: spill[:, t % SPILL, :]}[c]
                rope(v.rearrange("p (h d) -> p h d", d=HD), t, HA, roped)

            pool.wait_ge(s_sin, 4)

            def idx_rstd(n):
                pool.wait_ge(s_mi, n + 1)
                g.tensor_tensor(*(m[:, :].rearrange("p (j t) -> p j t", t=T)[:, :, slice(*IDX_TILES[n])]
                                  for m in (rs_i, ms_i, neg_half)), ALU.pow).then_inc(s_ri, 1)

            def idx_rope(t0, t1):
                for t in range(t0, t1):
                    pool.wait_ge(s_ni, t + 1)
                    rope(proji[:, t, 0:CI_IW].rearrange("p (h d) -> p h d", d=HD), t, IH + 1, roped_i)

            idx_rstd(0)
            for k in range(NSTAGE):
                w_low(CH_QA * KT + k)
            idx_rstd(1)
            idx_rope(0, 2)
            for k in range(NSTAGE, KT):
                w_low(CH_QA * KT + k)
            idx_rope(2, IDX_TILES[1][1])
            idx_rstd(2)
            idx_rope(IDX_TILES[1][1], T)
            for c in range(CH_QA, NIN):
                turned = c in (CH_QA, CH_KA, CH_QB)
                for t in range(6 if turned else 0):
                    rope_tile(c, t)
                for k in range(KT):
                    w_low((c + 1) * KT + k)
                    if c == CH_QA and k == KT - 1:
                        for t in SEL:
                            last = max(i for i, grp in enumerate(IDX_GROUPS) if grp[0] == t)
                            pool.wait_ge(s_isum, IH * (last + 1))
                            d = score[:, SOFF[t] + t * P:SOFF[t] + (t + 1) * P]
                            g.affine_select(out=d, in_=d, compare_op=ALU.is_ge, fill=FILL, base=0,
                                            pattern=[[-1, P]], channel_multiplier=1).then_inc(s_ifill, 1)
                for t in range(6, T if turned else 0):
                    rope_tile(c, t)
                if c == CH_VA:
                    pool.wait_ge(s_fa, freed(USE_AT[("kb",)])[0])
                    for t in range(T):
                        rope(kb[:, t, :, :], t, 2, roped_kb)
                    double(0)
            for head in range(1, HA):
                double(head)
            pool.wait_ge(s_on, HA)
            for t in range(T):
                pool.wait_ge(s_za[t % 2], 16 * (t // 2 + 1))
                g.tensor_tensor(qa[:, t, :], qa[:, t, :], za_in[:, t % 2, :], ALU.mult).then_inc(s_ya, 1)

            def y_rstd(n, cols, squares):
                pool.wait_ge(s_yss, squares)
                m = ms_y[:, cols]
                g.tensor_scalar(m, m, 1.0 / WIDTH, EPS, ALU.mult, ALU.add).then_inc(s_ym, 1)
                pool.wait_ge(s_ym, n + 1)
                rstd(rs_y[:, cols], m).then_inc(s_yr, 1)

            y_rstd(0, slice(0, T), T)
            for t in range(T):
                y_rstd(t + 1, slice(T + t, T + t + 1), T + t + 1)
                w_low(CH_OUT1 * KT + t)
            for t in range(T):
                pool.wait_ge(s_hm, t + 1)
                rstd(rs_o[:, t:t + 1], ms_o[:, T + t:T + t + 1]).then_inc(s_hr, 1)

        @block.scalar
        def _(act):
            a = nc.scalar

            def w_high(n):
                c, k = divmod(n, KT)
                raw, landed, count = w_landing(n)
                act.wait_ge(landed, count)
                gain = (ginT if c < NIN else gyT)[:, k:k + 1]
                a.activation(raw, raw, ACT.Copy, scale=gain).then_inc(s_wg, 1)
                act.wait_ge(s_wg, n + 1)
                if c == CH_OUT1:
                    act.wait_ge(s_pv, NU)
                elif c:
                    if k < KT - 1:
                        act.wait_ge(s_wused, (c - 1) * (KT - 1) + k + 1)
                    else:
                        act.wait_ge(s_proj, c * T)
                a.activation(w_split(c)[0][:, k, 0:CHUNK_W[c]], raw, ACT.Copy).then_inc(s_whi, 1)

            def part_high(name, dst):
                act.wait_ge(s_tr, USE_AT[name] + 1)
                a.activation(dst, tbank(name, slice(0, dst.shape[0])), ACT.Copy).then_inc(s_hi, 1)

            def bank_copy(name, dst):
                act.wait_ge(s_tr, USE_AT[name] + 1)
                a.activation(dst, tbank(name)[:, 0:dst.free_size()], ACT.Copy).then_inc(s_fa, 1)

            def squares(t):
                if t >= 2:
                    act.wait_ge(s_ss, t - 1)
                a.activation(xsq[:, t % 2, :], xraw[:, t, :], ACT.Square, accum_out=ms[:, t:t + 1])\
                    .then_inc(s_ss, 1)

            def x_high(t):
                for gg in range(2):
                    part_high(("x", t, gg), uhi[:, 4 * gg:4 * gg + 4, t * P:(t + 1) * P])

            act.wait_ge(s_fv, freed(USE_AT[("rows",)])[1])
            for t in range(2):
                w_high(2 * t)
                x_high(t)
                w_high(2 * t + 1)
            for k in range(4, KT):
                w_high(k)
            squares(0)
            squares(1)
            act.wait_ge(s_ang, 1)
            for j in range(2):
                a.activation(sind[:, :, j, :], ang[:, :, :], ACT.Sin).then_inc(s_sin, 1)
                a.activation(cosd[:, :, j, :], ang2[:, :, :], ACT.Sin).then_inc(s_sin, 1)

            def evac(c, t):
                act.wait_ge(s_proj, c * T + t + 1)
                fn, n = ACT.Copy, (c - CH_QB) * T + t
                if c == CH_IDX:
                    act.wait_ge(s_rs, t + 1)
                    dst = proji[:, t, :]
                elif c in (CH_QA, CH_KA):
                    dst = (qa if c == CH_QA else ka)[:, t, :]
                elif c == CH_VA:
                    act.wait_ge(s_isum, IH * len(IDX_GROUPS))
                    dst = va[:, t, :]
                else:
                    if n >= SPILL:
                        act.wait_ge(s_spill[n % SPILL], 16 * (n // SPILL))
                    dst = spill[:, n % SPILL, :]
                    fn = ACT.Copy if c == CH_QB else ACT.Silu
                a.activation(dst, proj_bank(c, t), fn, scale=rs[:, t:t + 1]).then_inc(s_pev, 1)

            def idx_step(name):
                if name[0] == "ckv":
                    bank_copy(name, ckvT[:, name[1] * 512:(name[1] + 1) * 512])
                elif name[0] == "kb":
                    act.wait_ge(s_tr, USE_AT[name] + 1)
                    src = tbank(name).rearrange("p (t d) -> p t d", d=HD).unsqueeze(2).to_broadcast([P, T, 2, HD])
                    a.activation(kb[:, :, :, :], src, ACT.Copy).then_inc(s_fa, 1)
                elif name[0] == "ik":
                    part_high(name, ikhi[:, name[1] * 512:(name[1] + 1) * 512])
                elif name[0] == "iq":
                    t = name[1]
                    if t - 2 in SEL:
                        last = max(i for i, grp in enumerate(IDX_GROUPS) if grp[0] == t - 2)
                        act.wait_ge(s_isc, IH * (last + 1))
                    part_high(name, iqst[0:HD, t % 2, :])
                else:
                    n, w = IH * name[1] + name[2], IDX_GROUPS[name[1]][2]
                    act.wait_ge(s_isc, n + 1)
                    if n >= 4:
                        act.wait_ge(s_isum, n - 3)
                    a.activation(relu[:, n % 4, 0:w], psum[:, 2 + n % 2, 0:w], ACT.Relu).then_inc(s_rel, 1)

            for c in range(NIN):
                for p in range(4):
                    for k in range(KT):
                        if k == (KT - 2 if p == 3 and c > CH_QA else KT - 1):
                            evac(c, 2 * p)
                            evac(c, 2 * p + 1)
                        if c == 0 and (p, k) in X_STEPS:
                            x_high(X_STEPS[p, k])
                            squares(X_STEPS[p, k])
                        if p == 3 and (c + 1) * KT + k < CH_OUT0 * KT + KT - 2:
                            w_high((c + 1) * KT + k)
                        for name in IDX_STEPS.get((c, p, k), ()):
                            idx_step(name)

            def side(name):
                kind, head = name[0], name[1]
                if kind == "kbt":
                    part_high(name, kbhi[:, head * 512:(head + 1) * 512])
                    return
                if kind == "ya":
                    part_high(name, yhi[0][:, :, head * P:(head + 1) * P])
                    return
                cols = slice(name[2] * 512, (name[2] + 1) * 512)
                if head >= 2:
                    act.wait_ge(s_sc, T * (head - 1))
                part_high(name, qst[0:HD, head % 2, cols] if kind == "q" else khi[:, head % 2, cols])

            def y_squares(b, t):
                n = b * T + t
                if b == 0:
                    act.wait_ge(s_ya, t + 1)
                if n >= 2:
                    act.wait_ge(s_yss, n - 1)
                a.activation(ysq[:, n % 2, :], (qa if b == 0 else qb)[:, t, :], ACT.Square,
                             accum_out=ms_y[:, n:n + 1]).then_inc(s_yss, 1)

            for name in prep_names(0):
                side(name)
            w_high(CH_OUT0 * KT + KT - 2)
            w_high(CH_OUT0 * KT + KT - 1)
            for i in range(NU + LAG_T):
                for name in side_uses(i):
                    side(name)
                if i >= LAG_T:
                    u = i - LAG_T
                    for n, (b, nb) in enumerate(PT_PARTS[u]):
                        if USES[USE_AT[("p", u, n)]][1] == "A":
                            if u >= PT_SLOTS:
                                act.wait_ge(s_pv, u - PT_SLOTS + 1)
                            bank_copy(("p", u, n), pt[:, u % PT_SLOTS, b * P:(b + nb) * P])
                if i < NU:
                    head, t = UNITS[i]
                    act.wait_ge(s_mk, i + 1)
                    v = sm[:, i % SM_SLOTS, 0:(t + 1) * P]
                    a.activation(v, v, ACT.Exp, bias=shift[:, i:i + 1], scale=-1.0,
                                 accum_out=denom[:, head, t:t + 1]).then_inc(s_ex, 1)
                    if head >= HA and i % T == T - 1:
                        y_squares(0, head - HA)
                for name in late_uses(i):
                    bank_copy(name, vb[:, name[1], :])

            def yb_high(t):
                part_high(("yb", t), yhi[1][:, :, t * P:(t + 1) * P])

            yb_high(0)
            yb_high(1)
            act.wait_ge(s_yb, HB)
            for t in range(T):
                if t >= 2:
                    yb_high(t)
                y_squares(1, t)
                w_high(CH_OUT1 * KT + t)
            for n in range(2 * T):
                c, t = divmod(n, T)
                act.wait_ge(s_h, n + 1)
                if n >= 2:
                    act.wait_ge(s_hs, n - 1)
                a.activation(ysq[:, n % 2, :], hres[c][:, t, :], ACT.Square, accum_out=ms_o[:, n:n + 1])\
                    .then_inc(s_hs, 1)

        @block.tensor
        def _(pe):
            te = nc.tensor

            def bank_free(name):
                before = USE_BEFORE[USE_AT[name]]
                if before is not None:
                    by_act, by_dve = freed(before)
                    if by_act:
                        pe.wait_ge(s_fa, by_act)
                    if by_dve:
                        pe.wait_ge(s_fv, by_dve)

            def turn(name, tiles):
                bank_free(name)
                b = tbank(name)
                for j, v in enumerate(tiles):
                    ins = te.matmul(b[0:v.shape[1], j * P:(j + 1) * P], v, ident[:, :], start=True, stop=True,
                                    is_transpose=True)
                ins.then_inc(s_tr, 1)

            def both(v):
                return v.rearrange("p a d -> p (a d)")

            def x_turn(t):
                pe.wait_ge(s_x[t], 16)
                for gg in range(2):
                    turn(("x", t, gg), [xraw[:, t, (4 * gg + j) * P:(4 * gg + j + 1) * P] for j in range(4)])

            def gains_turn():
                pe.wait_ge(s_gains, 32)
                bank_free(("gains",))
                te.matmul(tbank(("gains",))[:, 0:KT], gyr[:, :], ident[0:T, 0:T], start=True, stop=True,
                          is_transpose=True).then_inc(s_tr, 1)

            def pair(c, p, src_ready):
                q = c * 4 + p
                if q >= 2:
                    pe.wait_ge(s_pev, 2 * (q - 1))
                w = CHUNK_W[c]
                for k in range(KT):
                    if p == 0:
                        pe.wait_ge(s_wsplit, c * KT + k + 1)
                    for t in (2 * p, 2 * p + 1):
                        dst, cols = proj_bank(c, t), slice(t * P, (t + 1) * P)
                        if k == 0:
                            src_ready(t)
                        te.matmul(dst, uhi[:, k, cols], whi[:, k, 0:w], start=(k == 0), stop=False)
                        te.matmul(dst, uhi[:, k, cols], wlo[:, k, 0:w], start=False, stop=False)
                        ins = te.matmul(dst, ulo[:, k, cols], whi[:, k, 0:w], start=False, stop=(k == KT - 1))
                        if k == KT - 1:
                            ins.then_inc(s_proj, 1)
                        elif p == 3 and t == T - 1:
                            ins.then_inc(s_wused, 1)
                    if c == 0 and (p, k) in X_STEPS:
                        if (p, k) == min(X_STEPS):
                            gains_turn()
                        x_turn(X_STEPS[p, k])
                    for name in IDX_STEPS.get((c, p, k), ()):
                        idx_step(name)

            def idx_step(name):
                if name[0] == "ckv":
                    pe.wait_ge(s_ni, 4 * (name[1] + 1))
                    turn(name, [proji[:, 4 * name[1] + j, CI_CKV:IDXW] for j in range(4)])
                elif name[0] == "kb":
                    bank_free(name)
                    pe.wait_ge(s_fa, freed(USE_AT[("ckv", 1)])[0])
                    for t in range(T):
                        ins = te.matmul(tbank(name)[:, t * HD:(t + 1) * HD], ckvT[:, t * P:(t + 1) * P], uk[:, :],
                                        start=True, stop=True)
                    ins.then_inc(s_tr, 1)
                elif name[0] == "ik":
                    pe.wait_ge(s_ikd, 1)
                    turn(name, [both(ikdup[:, 4 * name[1] + j]) for j in range(4)])
                elif name[0] == "iq":
                    pe.wait_ge(s_roi, name[1] + 1)
                    turn(name, [proji[:, name[1], h * HD:(h + 1) * HD] for h in range(IH)])
                else:
                    _, i, h = name
                    t, k0, w = IDX_GROUPS[i]
                    n = IH * i + h
                    if k0 == 0 and h == 0:
                        pe.wait_ge(s_fv, freed(USE_AT[("iq", t)])[1])
                    if n >= 2:
                        pe.wait_ge(s_rel, n - 1)
                    dst, q = psum[:, 2 + n % 2, 0:w], iqst[:, t % 2, h * P:(h + 1) * P]
                    te.matmul(dst, q, ikhi[:, k0:k0 + w], start=True, stop=False)
                    te.matmul(dst, q, iklo[:, k0:k0 + w], start=False, stop=True).then_inc(s_isc, 1)

            pe.wait_ge(s_const, 3 + HALF + 3 + 1)
            pe.wait_ge(s_posf, 1)
            for n, v in enumerate((ginr, posf)):
                ins = te.matmul(tbank(("rows",))[:, n * T:(n + 1) * T], v[:, :], ident[0:T, 0:T], start=True,
                                stop=True, is_transpose=True)
            ins.then_inc(s_tr, 1)
            x_turn(0)
            x_turn(1)
            for c in range(NIN):
                for p in range(4):
                    pair(c, p, lambda t: pe.wait_ge(s_fv, freed(USE_AT[("x", t, 1)])[1]) if c == 0 else None)

            def b_values(name):
                bank_free(name)
                te.matmul(tbank(name), ckvT[:, name[1] * P:(name[1] + 1) * P],
                          uv[:, :, :].rearrange("p h d -> p (h d)"), start=True, stop=True).then_inc(s_tr, 1)

            def side(name):
                kind, head = name[0], name[1]
                if kind == "ya":
                    pe.wait_ge(s_ya, head + 1)
                    turn(name, [qa[:, head, j * P:(j + 1) * P] for j in range(4)])
                elif kind == "kbt":
                    pe.wait_ge(s_kbr, 4 * (head + 1))
                    turn(name, [both(kb[:, 4 * head + j]) for j in range(4)])
                else:
                    if head == HA and kind == "q":
                        pe.wait_ge(s_qb, 16)
                    if kind == "k":
                        pe.wait_ge(s_kd, head + 1)
                        twice = kdup[:, head % 2] if head else kdup0[:, :, :, :]
                        turn(name, [both(twice[:, 4 * name[2] + j]) for j in range(4)])
                        return
                    src = qa if head < HA else qb
                    cols = slice(head % HA * HD, (head % HA + 1) * HD)
                    turn(name, [src[:, 4 * name[2] + j, cols] for j in range(4)])

            def scores(i):
                head, t = UNITS[i]
                n = (t + 1) * P
                if i >= 2:
                    pe.wait_ge(s_mk, i - 1)
                if i % T == 0:
                    pe.wait_ge(s_fv, freed(USE_AT[prep_names(head)[-1]])[1])
                    if head == HA:
                        pe.wait_ge(s_fv, freed(USE_AT[("kbt", 1)])[1])
                q = qst[:, head % 2, t * P:(t + 1) * P]
                for k0 in range(0, n, 512):
                    w = min(512, n - k0)
                    dst = psum[:, 2 + 2 * (i % 2) + k0 // 512, 0:w]
                    hi = (khi[:, head % 2, :] if head < HA else kbhi)[:, k0:k0 + w]
                    lo = (klo[:, head % 2, :] if head < HA else kblo)[:, k0:k0 + w]
                    te.matmul(dst, q, hi, start=True, stop=False)
                    ins = te.matmul(dst, q, lo, start=False, stop=True)
                ins.then_inc(s_sc, 1)

            def p_turn(u):
                pe.wait_ge(s_ex, u + 1)
                for n, (b, nb) in enumerate(PT_PARTS[u]):
                    turn(("p", u, n), [sm[:, u % SM_SLOTS, (b + j) * P:(b + j + 1) * P] for j in range(nb)])

            def values(u):
                head, t = UNITS[u]
                by_act, by_dve = freed(USE_AT[("p", u, len(PT_PARTS[u]) - 1)])
                pe.wait_ge(s_fa, by_act)
                pe.wait_ge(s_fv, by_dve)
                if u % T == 0 and head >= 2:
                    pe.wait_ge(s_on, head - 1)
                v = va if head < HA else vb
                cols = slice(head % HA * HD, (head % HA + 1) * HD)
                dst = psum[:, OBANK[head % 2], t * HD:(t + 1) * HD]
                for b in range(t + 1):
                    ins = te.matmul(dst, pt[:, u % PT_SLOTS, b * P:(b + 1) * P], v[:, b, cols],
                                    start=(b == 0), stop=(b == t))
                ins.then_inc(s_pv, 1)

            pe.wait_ge(s_rope, 2 * T)
            for n, name in enumerate(prep_names(0)):
                if n == 2:
                    pe.wait_ge(s_pev, NIN * T)
                side(name)
            for i in range(NU + LAG_V):
                for name in side_uses(i):
                    side(name)
                if i < NU:
                    scores(i)
                for name in late_uses(i):
                    b_values(name)
                if LAG_T <= i < NU + LAG_T:
                    p_turn(i - LAG_T)
                if i >= LAG_V:
                    values(i - LAG_V)

            def yb_turn(t):
                if t == 0:
                    pe.wait_ge(s_yb, HB)
                turn(("yb", t), [qb[:, t, j * P:(j + 1) * P] for j in range(4)])

            def out_part(n, b):
                c, t = CH_OUT0 + n // T, n % T
                hi, lo = w_split(c)
                if b == 0 and n == 0:
                    pe.wait_ge(s_fv, freed(USE_AT[("ya", T - 1)])[1])
                if b == 0 and n == 2:
                    pe.wait_ge(s_on, HEADS)
                if b == 0 and n >= 3:
                    pe.wait_ge(s_h, n - 2)
                if b == 1 and c == CH_OUT0:
                    pe.wait_ge(s_fv, freed(USE_AT[("yb", t)])[1])
                dst, cols = psum[:, OUT_BANKS[n % 3][b], :], slice(t * P, (t + 1) * P)
                for j in range(KT // 2):
                    k = b * KT // 2 + j
                    if t == 0:
                        pe.wait_ge(s_wsplit, c * KT + k + 1)
                    te.matmul(dst, yhi[b][:, j, cols], hi[:, k, :], start=(j == 0), stop=False)
                    te.matmul(dst, yhi[b][:, j, cols], lo[:, k, :], start=False, stop=False)
                    ins = te.matmul(dst, ylo[b][:, j, cols], hi[:, k, :], start=False, stop=(j == KT // 2 - 1))
                if b == 1:
                    ins.then_inc(s_proj, 1)

            out_part(0, 0)
            out_part(1, 0)
            yb_turn(0)
            yb_turn(1)
            out_part(2, 0)
            out_part(0, 1)
            yb_turn(2)
            out_part(1, 1)
            yb_turn(3)
            for n in range(2, 2 * T):
                if n + 1 < 2 * T:
                    out_part(n + 1, 0)
                out_part(n, 1)
                if n + 2 < T:
                    yb_turn(n + 2)

        @block.vector
        def _(dve):
            v = nc.vector
            n_steps = [0]

            def step(ins):
                n_steps[0] += 1
                ins.then_inc(s_v, 1)
                dve.wait_ge(s_v, n_steps[0])

            def part_low(name, dst, hi, lanes=slice(0, P)):
                dve.wait_ge(s_hi, rounded(USE_AT[name]))
                v.tensor_tensor(dst, tbank(name, lanes), hi.bitcast(F32), ALU.subtract).then_inc(s_fv, 1)

            dve.wait_ge(s_rows, 32)
            v.tensor_copy(posf[:, :], posr[:, :]).then_inc(s_posf, 1)
            dve.wait_ge(s_tr, USE_AT[("rows",)] + 1)
            v.tensor_copy(ginT[:, :], tbank(("rows",))[:, 0:T])
            v.tensor_copy(post[:, :], tbank(("rows",))[:, T:2 * T]).then_inc(s_fv, 1)

            def x_mean(t):
                dve.wait_ge(s_ss, t + 1)
                v.tensor_scalar(ms[:, t:t + 1], ms[:, t:t + 1], 1.0 / D, EPS, ALU.mult, ALU.add)\
                    .then_inc(s_mean, 1)

            def u_low(t):
                for gg in range(2):
                    cols = slice(t * P, (t + 1) * P)
                    part_low(("x", t, gg), ulo[:, 4 * gg:4 * gg + 4, cols], uhi[:, 4 * gg:4 * gg + 4, cols])

            def angles():
                flat = [P, T * HALF]
                dve.wait_ge(s_fv, freed(USE_AT[("rows",)])[1])
                dve.wait_ge(s_const, 3 + HALF)
                step(v.tensor_tensor(ang[:, :, :], post[:, :].unsqueeze(2).to_broadcast([P, T, HALF]),
                                     freq[:, :].unsqueeze(1).to_broadcast([P, T, HALF]), ALU.mult))
                step(v.tensor_scalar(turns[:, :, :], ang[:, :, :], 1.0 / (2 * math.pi), None, ALU.mult))
                step(v.tensor_copy(turni[:, :, :], turns[:, :, :]))
                step(v.tensor_copy(turns[:, :, :], turni[:, :, :]))
                c1 = 6.28125
                c2 = float(np.float32(np.round((2 * math.pi - c1) * 2 ** 20) / 2 ** 20))
                c3 = 2 * math.pi - c1 - c2
                for part in (c1, c2, c3):
                    step(v.scalar_tensor_tensor(ang[:, :, :], turns[:, :, :], -part, ang[:, :, :],
                                                ALU.mult, ALU.add))
                top = float(np.float32(3.1415925))
                step(v.tensor_scalar(ang[:, :, :], ang[:, :, :], top, -top, ALU.min, ALU.max))
                step(v.tensor_scalar(turns[:, :, :], ang[:, :, :], -1.0, None, ALU.mult))
                step(v.tensor_tensor(ang2[:, :, :], ang[:, :, :], turns[:, :, :], ALU.max))
                v.tensor_scalar(ang2[:, :, :], ang2[:, :, :], -1.0, math.pi / 2, ALU.mult, ALU.add)\
                    .then_inc(s_ang, 1)

            def strip_pattern(n):
                window, dilation = PATTERNS[n]
                step(v.tensor_scalar(resid[:, :], dist[:, :], dilation - 1, None, ALU.bitwise_and))
                step(v.tensor_scalar(hit[:, :], resid[:, :], 0.0, None, ALU.is_equal))
                if n == 0:
                    step(v.scalar_tensor_tensor(mult[:, :], dist[:, :], float(window), hit[:, :],
                                                ALU.is_le, ALU.mult))
                else:
                    step(v.scalar_tensor_tensor(hit[:, :], dist[:, :], float(window), hit[:, :],
                                                ALU.is_le, ALU.mult))
                    step(v.tensor_tensor(mult[:, :], mult[:, :], hit[:, :], ALU.add))

            def strip_end():
                step(v.scalar_tensor_tensor(mult[:, :], dist[:, :], 0.0, mult[:, :], ALU.is_ge, ALU.mult))
                step(v.tensor_scalar(strip[:, :], mult[:, :], 0.0, -BIG, ALU.is_equal, ALU.mult))
                for m in range(2, len(PATTERNS) + 1):
                    step(v.tensor_scalar(hit[:, :], mult[:, :], float(m), math.log(m) / SCALE,
                                         ALU.is_equal, ALU.mult))
                    step(v.tensor_tensor(strip[:, :], strip[:, :], hit[:, :], ALU.add))

            u_low(0)
            u_low(1)
            dve.wait_ge(s_tr, USE_AT[("gains",)] + 1)
            v.tensor_copy(gyT[:, :], tbank(("gains",))[:, 0:KT]).then_inc(s_fv, 1)
            angles()
            x_mean(0)
            x_mean(1)
            dve.wait_ge(s_const, 3 + HALF + 3 + 3)
            for p in range(T // 2 - 1):
                u_low(2 * p + 2)
                u_low(2 * p + 3)
                x_mean(2 * p + 2)
                x_mean(2 * p + 3)
                if p < 2:
                    strip_pattern(p)

            for n, (t0, t1) in enumerate(IDX_TILES):
                if n == 2:
                    strip_pattern(2)
                    strip_end()
                for t in range(t0, t1):
                    dve.wait_ge(s_pev, t + 1)
                    for j, (c0, c1) in enumerate(((CI_CKV, IDXW), (CI_IK, CI_IW))):
                        col = proji[:, t, c0:c1]
                        step(v.tensor_tensor_reduce(out=junk[:, 0:c1 - c0], in0=col, in1=col, scale=1.0,
                                                    scalar=0.0, op0=ALU.mult, op1=ALU.add,
                                                    accum_out=ms_i[:, j * T + t:j * T + t + 1]))
                m = ms_i[:, t0:t1]
                v.tensor_scalar(m, m, 1.0 / LAT, EPS, ALU.mult, ALU.add)
                m = ms_i[:, T + t0:T + t1]
                v.tensor_scalar(m, m, 1.0 / HD, EPS, ALU.mult, ALU.add).then_inc(s_mi, 1)
                dve.wait_ge(s_ri, n + 1)
                if n == 0:
                    dve.wait_ge(s_small, 64)
                for t in range(t0, t1):
                    ckv, ik = proji[:, t, CI_CKV:IDXW], proji[:, t, CI_IK:CI_IW]
                    v.scalar_tensor_tensor(ckv, ckv, rs_i[:, t:t + 1], g_kv[:, :], ALU.mult, ALU.mult)
                    v.scalar_tensor_tensor(ik, ik, rs_i[:, T + t:T + t + 1], g_ik[:, :], ALU.mult, ALU.mult)\
                        .then_inc(s_ni, 1)
            step(v.tensor_scalar(iw[:, :, :], proji[:, :, CI_IW:CI_CKV], IH ** -0.5 * HD ** -0.5, None, ALU.mult))

            dve.wait_ge(s_roi, T)
            v.tensor_copy(ikdup[:, :, :, :], proji[:, :, CI_IK:CI_IW].unsqueeze(2).to_broadcast([P, T, 2, HD]))\
                .then_inc(s_ikd, 1)

            for key in sorted(IDX_STEPS):
                for name in IDX_STEPS[key]:
                    if name[0] == "ik":
                        cols = slice(name[1] * 512, (name[1] + 1) * 512)
                        part_low(name, iklo[:, cols], ikhi[:, cols])
                    elif name[0] == "iq":
                        q = iqst[:, name[1] % 2, :]
                        part_low(name, q[HD:P], q[0:HD], slice(0, HD))
                    elif name[0] == "score":
                        _, i, h = name
                        t, k0, w = IDX_GROUPS[i]
                        n = IH * i + h
                        dst = score[:, SOFF[t] + k0:SOFF[t] + k0 + w]
                        dve.wait_ge(s_rel, n + 1)
                        r, wt = relu[:, n % 4, 0:w], iw[:, t, h:h + 1]
                        if h == 0:
                            v.tensor_scalar(dst, r, wt, None, ALU.mult).then_inc(s_isum, 1)
                        else:
                            dve.wait_ge(s_isum, n)
                            v.scalar_tensor_tensor(dst, r, wt, dst, ALU.mult, ALU.add).then_inc(s_isum, 1)

            dve.wait_ge(s_ifill, NSEL)

            def rows(t):
                return slice(SOFF[t], SOFF[t] + (t + 1) * P)

            def count(op, threshold):
                for j, t in enumerate(SEL):
                    ins = v.tensor_scalar(hits[:, rows(t)], score[:, rows(t)], threshold(j), None, op, ALU.add,
                                          accum_out=cnt[:, j:j + 1])
                return ins

            def candf(j):
                return cand[:, j:j + 1].bitcast(F32)

            step(count(ALU.is_ge, lambda j: 0.0))
            step(v.tensor_scalar(neg[:, :], cnt[:, :], float(TOPK), None, ALU.is_lt))
            step(v.tensor_scalar(negi[:, :], cnt[:, :], float(TOPK), None, ALU.is_lt))
            step(v.tensor_scalar(sgn[:, :], negi[:, :], 31, None, ALU.logical_shift_left))

            def test_bit(steps_before):
                v.scalar_tensor_tensor(cand[:, :], mag[:, :], bit[:, 0:1], sgn[:, :],
                                       ALU.bitwise_or, ALU.bitwise_or).then_inc(s_tk, 1)
                dve.wait_ge(s_tk, steps_before + 1)
                count(ALU.is_ge, candf).then_inc(s_tk, 1)
                dve.wait_ge(s_tk, steps_before + 2)
                v.scalar_tensor_tensor(acc[:, :], cnt[:, :], float(TOPK), neg[:, :],
                                       ALU.is_ge, ALU.not_equal).then_inc(s_tk, 1)
                dve.wait_ge(s_tk, steps_before + 3)
                v.scalar_tensor_tensor(mag[:, :], acc[:, :], bit[:, 1:2], mag[:, :],
                                       ALU.logical_shift_left, ALU.bitwise_or)
                v.tensor_scalar(bit[:, 0:1], bit[:, 0:1], 1, None, ALU.logical_shift_right)
                v.tensor_scalar(bit[:, 1:2], bit[:, 1:2], -1.0, None, ALU.add).then_inc(s_tk, 1)
                dve.wait_ge(s_tk, steps_before + 4)

            test_bit(0)
            with dve.Fori(0, 6) as it:
                for b in range(5):
                    test_bit(it * 20 + 4 * (b + 1))
            step(v.tensor_tensor(mag[:, :], mag[:, :], negi[:, :], ALU.add))
            step(v.tensor_tensor(cand[:, :], mag[:, :], sgn[:, :], ALU.bitwise_or))

            def tie_step(n):
                j, part = divmod(n, TIE_PARTS)
                part -= 1
                w, s = (SEL[j] + 1) * P, score[:, rows(SEL[j])]
                if n == 0:
                    dve.wait_ge(s_wsplit, (NIN + 1) * KT)
                if part == -1:
                    step(v.tensor_scalar(rank[:, 0:w], s, candf(j), None, ALU.is_gt, ALU.add,
                                         accum_out=cnt[:, j:j + 1]))
                    step(v.tensor_scalar(need[:, j:j + 1], cnt[:, j:j + 1], -1.0, float(TOPK),
                                         ALU.mult, ALU.add))
                elif part == 0:
                    step(v.tensor_scalar(eq[:, 0:w], s, candf(j), None, ALU.is_equal))
                elif part == 1:
                    step(v.tensor_tensor_scan(rank[:, 0:w], eq[:, 0:w], eq[:, 0:w], 0.0, ALU.add, ALU.max))
                elif part == 2:
                    step(v.scalar_tensor_tensor(eq[:, 0:w], rank[:, 0:w], need[:, j:j + 1], eq[:, 0:w],
                                                ALU.is_le, ALU.mult))
                elif part == 3:
                    step(v.scalar_tensor_tensor(s, s, candf(j), eq[:, 0:w], ALU.is_gt, ALU.add))
                else:
                    step(v.tensor_scalar(s, s, BIG, -BIG, ALU.mult, ALU.add))

            def y_low(name, b, t):
                cols = slice(t * P, (t + 1) * P)
                part_low(name, ylo[b][:, :, cols], yhi[b][:, :, cols])

            def side(name):
                kind, head = name[0], name[1]
                if kind == "kbt":
                    cols = slice(head * 512, (head + 1) * 512)
                    part_low(name, kblo[:, cols], kbhi[:, cols])
                    return
                if kind == "ya":
                    y_low(name, 0, head)
                    return
                cols = slice(name[2] * 512, (name[2] + 1) * 512)
                if kind == "q":
                    q = qst[:, head % 2, cols]
                    part_low(name, q[HD:P], q[0:HD], slice(0, HD))
                else:
                    part_low(name, klo[:, head % 2, cols], khi[:, head % 2, cols])

            def mask(i):
                head, t = UNITS[i]
                n = (t + 1) * P
                dve.wait_ge(s_sc, i + 1)
                if i >= SM_SLOTS:
                    dve.wait_ge(s_tr, USE_AT[("p", i - SM_SLOTS, len(PT_PARTS[i - SM_SLOTS]) - 1)] + 1)
                b = 2 + 2 * (i % 2)
                src = psum[:, b:b + 2, :].rearrange("p a b -> p (a b)")[:, 0:n]
                v.tensor_tensor_reduce(out=sm[:, i % SM_SLOTS, 0:n], in0=src, in1=mask_of(head, t), scale=-SCALE,
                                       scalar=3e38, op0=ALU.add, op1=ALU.min,
                                       accum_out=shift[:, i:i + 1]).then_inc(s_mk, 1)

            def normalise(head):
                dve.wait_ge(s_pv, T * (head + 1))
                dve.wait_ge(s_ex, T * (head + 1))
                v.reciprocal(rden[:, head, :], denom[:, head, :]).then_inc(s_rd, 1)
                dve.wait_ge(s_rd, head + 1)
                dst = (qa if head < HA else qb)[:, :, head % HA * HD:(head % HA + 1) * HD]
                src = psum[:, OBANK[head % 2], :].rearrange("p (t d) -> p t d", d=HD)
                v.tensor_tensor(dst, src, rden[:, head, :].unsqueeze(2).to_broadcast([P, T, HD]), ALU.mult)\
                    .then_inc(s_on, 1)
                if head >= HA:
                    m = head - HA
                    dve.wait_ge(s_on, head + 1)
                    dve.wait_ge(s_zb[m % 2], 16 * (m // 2 + 1))
                    v.tensor_tensor(dst, dst, zb_in[:, m % 2, :, :], ALU.mult).then_inc(s_yb, 1)

            for name in prep_names(0):
                side(name)
            for i in range(NU + LAG_T):
                for name in side_uses(i):
                    side(name)
                if i < NU:
                    mask(i)
                if i >= LAG_T:
                    u = i - LAG_T
                    for n, (b, nb) in enumerate(PT_PARTS[u]):
                        name = ("p", u, n)
                        if USES[USE_AT[name]][1] == "V":
                            dve.wait_ge(s_tr, USE_AT[name] + 1)
                            if u >= PT_SLOTS:
                                dve.wait_ge(s_pv, u - PT_SLOTS + 1)
                            v.tensor_copy(pt[:, u % PT_SLOTS, b * P:(b + nb) * P], tbank(name)[:, 0:nb * P])\
                                .then_inc(s_fv, 1)
                if i in TIE_AT:
                    tie_step(TIE_AT[i])
                if i >= T + LAG_V and (i - LAG_V) % T == 0:
                    normalise((i - LAG_V) // T - 1)
            normalise(HEADS - 1)

            def residual(n):
                c, t = divmod(n, T)
                dve.wait_ge(s_proj, NIN * T + n + 1)
                if t % 2 == 0:
                    dve.wait_ge(s_xr[c][t // 2], 16)
                if c == 0:
                    dve.wait_ge(s_yr, t + 2)
                d = hres[c][:, t, :]
                part_a, part_b = (psum[:, bank, :] for bank in OUT_BANKS[n % 3])
                v.scalar_tensor_tensor(d, part_a, rs_y[:, t:t + 1], d, ALU.mult, ALU.add).then_inc(s_h0, 1)
                dve.wait_ge(s_h0, n + 1)
                v.scalar_tensor_tensor(d, part_b, rs_y[:, T + t:T + t + 1], d, ALU.mult, ALU.add).then_inc(s_h, 1)

            y_low(("yb", 0), 1, 0)
            y_low(("yb", 1), 1, 1)
            for t in range(T):
                residual(t)
                if t + 2 < T:
                    y_low(("yb", t + 2), 1, t + 2)
            dve.wait_ge(s_hs, T)
            step(v.tensor_scalar(ms_o[:, 0:T], ms_o[:, 0:T], 1.0 / D, EPS, ALU.mult, ALU.add))
            dve.wait_ge(s_gend, 16)
            for t in range(T):
                residual(T + t)
                dve.wait_ge(s_hs, T + t + 1)
                m = ms_o[:, T + t:T + t + 1]
                v.scalar_tensor_tensor(m, m, 1.0 / D, ms_o[:, t:t + 1], ALU.mult, ALU.add).then_inc(s_hm, 1)
                dve.wait_ge(s_hr, t + 1)
                for c in range(2):
                    v.scalar_tensor_tensor(hres[c][:, t, :], hres[c][:, t, :], rs_o[:, t:t + 1],
                                           fgain[:, c * 512:(c + 1) * 512], ALU.mult, ALU.mult).then_inc(s_res, 1)


_INS = ["x", "positions", "norm_in_gain", "w_in", "kv_norm_gain", "w_uk", "w_uv", "idx_k_norm_gain",
        "branch_norm_gain_a", "branch_norm_gain_b", "w_out", "final_norm_gain"]


def kernel(**inputs):
    import numpy as _np
    import concourse.bacc as _bacc
    from concourse import mybir as _mybir
    from concourse.bass_utils import run_bass_kernel_spmd as _run

    nc = _bacc.Bacc("TRN2", target_bir_lowering=False, num_devices=1)
    arrays, args = {}, []
    for name in _INS:
        a = _np.ascontiguousarray(inputs[name])
        arrays[f"in_{name}"] = a
        args.append(nc.dram_tensor(f"in_{name}", a.shape, _mybir.dt.from_np(a.dtype), kind="ExternalInput").ap())
    args.append(nc.dram_tensor("out", (1, SEQ, D), F32, kind="ExternalOutput").ap())
    hybrid_layer(nc, *args)
    r = _run(nc, [arrays], core_ids=[0])
    return r.results[0]["out"]
```
